# Optimizing a Trainium2 kernel written in Bass

```python
import jax, jax.numpy as jnp
from jax import lax
import numpy as np

D_MODEL = 1024
BATCH = 1
SEQ = 512
DEPTH = 1

MEM_LEN = 256
EPS = 1e-6
ATTN_HEADS = 8
ATTN_KV_HEADS = 2
ATTN_HEAD_DIM = 64
ATTN_GROUP = ATTN_HEADS // ATTN_KV_HEADS
WINDOW = 128
ATTN_BLOCK = 128
ROPE_THETA = 10000.0
DN_HEADS = 4
DN_HEAD_K = 128
DN_HEAD_V = 128
DN_CONV = 5
DN_CHUNK = 64
N_DIRS = 2
CROSS_HEADS = 4
CROSS_HEAD_DIM = D_MODEL // CROSS_HEADS
D_FF = -(-8 * D_MODEL // (3 * 256)) * 256
ATTN_WIDTH = ATTN_HEADS * ATTN_HEAD_DIM
DN_WIDTH = DN_HEADS * DN_HEAD_V
MIX_WIDTH = ATTN_WIDTH + DN_WIDTH
DN_QKV = DN_HEADS * (2 * DN_HEAD_K + DN_HEAD_V)
IN_SIZES = [ATTN_WIDTH, ATTN_KV_HEADS * ATTN_HEAD_DIM, ATTN_KV_HEADS * ATTN_HEAD_DIM,
            DN_QKV, DN_WIDTH, N_DIRS * DN_HEADS, N_DIRS * DN_HEADS]
IN_COLS = int(np.sum(IN_SIZES))
IN_SPLITS = [int(v) for v in np.cumsum(IN_SIZES)[:-1]]


def _rms_norm(x, gain):
    xf = x.astype(jnp.float32)
    y = xf * lax.rsqrt(jnp.mean(xf * xf, axis=-1, keepdims=True) + EPS)
    return (y * gain.astype(jnp.float32)).astype(x.dtype)

def _l2norm(x):
    return x * lax.rsqrt(jnp.sum(x * x, axis=-1, keepdims=True) + EPS)

def _rope(x, positions):
    half = x.shape[-1] // 2
    inv_freq = ROPE_THETA ** (-jnp.arange(half, dtype=jnp.float32) / half)
    ang = positions.astype(jnp.float32)[..., None] * inv_freq
    cos = jnp.cos(ang)[:, :, None, :]
    sin = jnp.sin(ang)[:, :, None, :]
    xf = x.astype(jnp.float32)
    x1, x2 = xf[..., :half], xf[..., half:]
    return jnp.concatenate([x1 * cos - x2 * sin, x2 * cos + x1 * sin], axis=-1)

def _window_attention(q, k, v, sink):
    b, s = q.shape[0], q.shape[1]
    nb = s // ATTN_BLOCK
    qb = q.reshape(b, nb, ATTN_BLOCK, ATTN_KV_HEADS, ATTN_GROUP, ATTN_HEAD_DIM)

    def band(t):
        tp = t.reshape(b, nb, ATTN_BLOCK, ATTN_KV_HEADS, ATTN_HEAD_DIM)
        tp = jnp.pad(tp, ((0, 0), (1, 1), (0, 0), (0, 0), (0, 0)))
        return jnp.concatenate([tp[:, :-2], tp[:, 1:-1], tp[:, 2:]], axis=2)

    kw, vw = band(k), band(v)
    scores = jnp.einsum('bnqhgd,bnkhd->bnhgqk', qb, kw) * (ATTN_HEAD_DIM ** -0.5)
    qi = jnp.arange(ATTN_BLOCK)[:, None]
    ki = jnp.arange(3 * ATTN_BLOCK)[None, :]
    in_band = jnp.abs(ki - ATTN_BLOCK - qi) <= WINDOW
    kpos = (jnp.arange(nb)[:, None] - 1) * ATTN_BLOCK + jnp.arange(3 * ATTN_BLOCK)[None, :]
    in_seq = (kpos >= 0) & (kpos < s)
    mask = in_band[None, :, :] & in_seq[:, None, :]
    scores = jnp.where(mask[None, :, None, None], scores, -jnp.inf)
    sk = sink.astype(jnp.float32).reshape(ATTN_KV_HEADS, ATTN_GROUP)[None, None, :, :, None, None]
    m = jnp.maximum(jnp.max(scores, axis=-1, keepdims=True), sk)
    p = jnp.exp(scores - m)
    denom = jnp.sum(p, axis=-1, keepdims=True) + jnp.exp(sk - m)
    o = jnp.einsum('bnhgqk,bnkhd->bnqhgd', p / denom, vw)
    return o.reshape(b, s, ATTN_WIDTH)

def _gated_delta_chunked(q, k, v, g, beta):
    b, h, s, dk = q.shape
    dv = v.shape[-1]
    c = DN_CHUNK
    n = s // c
    q = q.reshape(b, h, n, c, dk)
    k = k.reshape(b, h, n, c, dk)
    v = v.reshape(b, h, n, c, dv)
    g = jnp.cumsum(g.reshape(b, h, n, c), axis=-1)
    beta = beta.reshape(b, h, n, c)
    incl = jnp.tril(jnp.ones((c, c), dtype=bool))
    strict = jnp.tril(jnp.ones((c, c), dtype=bool), k=-1)
    decay = jnp.exp(jnp.where(incl, g[..., :, None] - g[..., None, :], -jnp.inf))
    kb = k * beta[..., None]
    lower = jnp.where(strict, jnp.einsum('bhnid,bhnjd->bhnij', kb, k) * decay, 0.0)
    tmat = lower + jnp.eye(c, dtype=jnp.float32)
    rhs = jnp.concatenate([v * beta[..., None], kb * jnp.exp(g)[..., None]], axis=-1)
    sol = lax.linalg.triangular_solve(tmat, rhs, left_side=True, lower=True, unit_diagonal=True)
    u, w = sol[..., :dv], sol[..., dv:]
    qk = jnp.einsum('bhnid,bhnjd->bhnij', q, k) * decay
    qg = q * jnp.exp(g)[..., None]
    kg = k * jnp.exp(g[..., -1:] - g)[..., None]
    g_last = jnp.exp(g[..., -1])

    def step(state, inp):
        qg_i, kg_i, u_i, w_i, qk_i, gl_i = inp
        v_new = u_i - jnp.einsum('bhck,bhkv->bhcv', w_i, state)
        o_i = jnp.einsum('bhck,bhkv->bhcv', qg_i, state) + jnp.einsum('bhij,bhjv->bhiv', qk_i, v_new)
        state = state * gl_i[..., None, None] + jnp.einsum('bhck,bhcv->bhkv', kg_i, v_new)
        return state, o_i

    xs = tuple(jnp.moveaxis(t, 2, 0) for t in (qg, kg, u, w, qk, g_last))
    state0 = jnp.zeros((b, h, dk, dv), jnp.float32)
    _, o = lax.scan(step, state0, xs)
    return jnp.moveaxis(o, 0, 2).reshape(b, h, s, dv)

def _gated_deltanet(qkv, gate, a, bt, conv_w, a_log, dt_bias, g_out):
    b, s = qkv.shape[0], qkv.shape[1]
    ch = qkv.shape[-1]
    pad = DN_CONV // 2
    conv = lax.conv_general_dilated(qkv, conv_w.reshape(DN_CONV, 1, ch).astype(qkv.dtype),
                                    window_strides=(1,), padding=[(pad, pad)],
                                    dimension_numbers=('NWC', 'WIO', 'NWC'), feature_group_count=ch)
    conv = jax.nn.silu(conv.astype(jnp.float32))
    nq = DN_HEADS * DN_HEAD_K
    q = conv[..., :nq].reshape(b, s, DN_HEADS, DN_HEAD_K)
    k = conv[..., nq:2 * nq].reshape(b, s, DN_HEADS, DN_HEAD_K)
    v = conv[..., 2 * nq:].reshape(b, s, DN_HEADS, DN_HEAD_V)
    q = (_l2norm(q) * (DN_HEAD_K ** -0.5)).transpose(0, 2, 1, 3)
    k = _l2norm(k).transpose(0, 2, 1, 3)
    v = v.transpose(0, 2, 1, 3)
    a = a.astype(jnp.float32).reshape(b, s, N_DIRS, DN_HEADS)
    bt = bt.astype(jnp.float32).reshape(b, s, N_DIRS, DN_HEADS)
    g = -jnp.exp(a_log.astype(jnp.float32)) * jax.nn.softplus(a + dt_bias.astype(jnp.float32))
    g = g.transpose(2, 0, 3, 1)
    beta = jax.nn.sigmoid(bt).transpose(2, 0, 3, 1)
    o_fwd = _gated_delta_chunked(q, k, v, g[0], beta[0])
    flip = lambda t: jnp.flip(t, axis=2)
    o_bwd = flip(_gated_delta_chunked(flip(q), flip(k), flip(v), flip(g[1]), flip(beta[1])))
    o = (o_fwd + o_bwd).transpose(0, 2, 1, 3)
    o = o * lax.rsqrt(jnp.mean(o * o, axis=-1, keepdims=True) + EPS) * g_out.astype(jnp.float32)
    o = o * jax.nn.silu(gate.astype(jnp.float32).reshape(b, s, DN_HEADS, DN_HEAD_V))
    return o.reshape(b, s, DN_WIDTH)

def _memory_cross_attention(h, mem_n, w_q, w_kv, w_o):
    b, s = h.shape[0], h.shape[1]
    m = mem_n.shape[1]
    q = (h @ w_q).reshape(b, s, CROSS_HEADS, CROSS_HEAD_DIM).astype(jnp.float32)
    kv = mem_n @ w_kv
    k = kv[..., :D_MODEL].reshape(b, m, CROSS_HEADS, CROSS_HEAD_DIM).astype(jnp.float32)
    v = kv[..., D_MODEL:].reshape(b, m, CROSS_HEADS, CROSS_HEAD_DIM).astype(jnp.float32)
    p = jax.nn.softmax(jnp.einsum('bqhd,bkhd->bhqk', q, k) * (CROSS_HEAD_DIM ** -0.5), axis=-1)
    o = jnp.einsum('bhqk,bkhd->bqhd', p, v).reshape(b, s, D_MODEL).astype(h.dtype)
    return o @ w_o

def _swiglu(h, w_gate_up, w_down):
    gu = h @ w_gate_up
    return (jax.nn.silu(gu[..., :D_FF]) * gu[..., D_FF:]) @ w_down

def first_inputs(seed: int = 0) -> dict:
    key = jax.random.key(seed)
    ks = jax.random.split(key, 24)
    f32 = jnp.float32

    def dense(k, fan_in, fan_out):
        return jax.random.normal(k, (DEPTH, fan_in, fan_out), f32) * fan_in ** -0.5

    def gain(k, n):
        return 1.0 + 0.02 * jax.random.normal(k, (DEPTH, n), f32)

    x = jax.random.normal(ks[0], (BATCH, SEQ, D_MODEL), f32)
    mem = jax.random.normal(ks[1], (BATCH, MEM_LEN, D_MODEL), f32)
    offsets = jax.random.randint(ks[2], (BATCH, 1), 0, 4096, dtype=jnp.int32)
    positions = jnp.arange(SEQ, dtype=jnp.int32)[None, :] + offsets
    dt = jnp.exp(jax.random.uniform(ks[3], (DEPTH, N_DIRS, DN_HEADS), f32)
                 * (np.log(0.1) - np.log(0.001)) + np.log(0.001))
    return {
        'x': x,
        'mem': mem,
        'positions': positions,
        'g_mix_pre': gain(ks[4], D_MODEL),
        'w_in': dense(ks[5], D_MODEL, IN_COLS),
        'conv_w': jax.random.normal(ks[6], (DEPTH, DN_CONV, DN_QKV), f32) * DN_CONV ** -0.5,
        'a_log': jnp.log(jax.random.uniform(ks[7], (DEPTH, N_DIRS, DN_HEADS), f32, 1.0, 16.0)),
        'dt_bias': dt + jnp.log(-jnp.expm1(-dt)),
        'g_dn_out': gain(ks[8], DN_HEAD_V),
        'attn_sink': 0.5 * jax.random.normal(ks[9], (DEPTH, ATTN_HEADS), f32),
        'w_out': dense(ks[10], MIX_WIDTH, D_MODEL),
        'g_mix_post': gain(ks[11], D_MODEL),
        'g_cross_pre': gain(ks[12], D_MODEL),
        'g_mem': gain(ks[13], D_MODEL),
        'w_cq': dense(ks[14], D_MODEL, D_MODEL),
        'w_ckv': dense(ks[15], D_MODEL, 2 * D_MODEL),
        'w_co': dense(ks[16], D_MODEL, D_MODEL),
        'g_cross_post': gain(ks[17], D_MODEL),
        'g_ffn_pre': gain(ks[18], D_MODEL),
        'w_gate_up': dense(ks[19], D_MODEL, 2 * D_FF),
        'w_down': dense(ks[20], D_FF, D_MODEL),
        'g_ffn_post': gain(ks[21], D_MODEL),
    }

def first_block(x, mem, positions, g_mix_pre, w_in, conv_w, a_log, dt_bias, g_dn_out, attn_sink,
              w_out, g_mix_post, g_cross_pre, g_mem, w_cq, w_ckv, w_co, g_cross_post,
              g_ffn_pre, w_gate_up, w_down, g_ffn_post):
    b, s = x.shape[0], x.shape[1]
    for l in range(DEPTH):
        h = _rms_norm(x, g_mix_pre[l])
        proj = h @ w_in[l]
        aq, ak, av, dqkv, dgate, dalpha, dbeta = jnp.split(proj, IN_SPLITS, axis=-1)
        aq = _rope(aq.reshape(b, s, ATTN_HEADS, ATTN_HEAD_DIM), positions)
        ak = _rope(ak.reshape(b, s, ATTN_KV_HEADS, ATTN_HEAD_DIM), positions)
        av = av.reshape(b, s, ATTN_KV_HEADS, ATTN_HEAD_DIM).astype(jnp.float32)
        attn_o = _window_attention(aq, ak, av, attn_sink[l]).astype(x.dtype)
        dn_o = _gated_deltanet(dqkv, dgate, dalpha, dbeta, conv_w[l], a_log[l], dt_bias[l],
                               g_dn_out[l]).astype(x.dtype)
        mix = jnp.concatenate([attn_o, dn_o], axis=-1) @ w_out[l]
        x = x + _rms_norm(mix, g_mix_post[l])
        c = _memory_cross_attention(_rms_norm(x, g_cross_pre[l]), _rms_norm(mem, g_mem[l]),
                                    w_cq[l], w_ckv[l], w_co[l])
        x = x + _rms_norm(c, g_cross_post[l])
        f = _swiglu(_rms_norm(x, g_ffn_pre[l]), w_gate_up[l], w_down[l])
        x = x + _rms_norm(f, g_ffn_post[l])
    return x


DEPTH_2 = 2

HEAD_DIM = 64
N_HEADS = 16
DIL_WINDOWS = (128, 512, 2048)
DIL_RATES = (1, 4, 16)
N_DIL = 3
N_KV_HEADS = 2
CMP_STRIDE = 16
CMP_LEN = 32
CMP_HIDDEN = 128
SEL_BLOCK = 64
N_SELECT = 16
SLIDE_WINDOW = 512
D_FF_2 = 2816
Q_BLOCK = 128


def rms_norm(x, g):
    xf = x.astype(jnp.float32)
    y = xf * lax.rsqrt(jnp.mean(xf * xf, axis=-1, keepdims=True) + EPS)
    return (y * g.astype(jnp.float32)).astype(x.dtype)

def modulate(x, shift, scale):
    return x * (1.0 + scale) + shift

def rope(x):
    s = x.shape[1]
    half = HEAD_DIM // 2
    inv = ROPE_THETA ** (-jnp.arange(half, dtype=jnp.float32) / half)
    ang = jnp.arange(s, dtype=jnp.float32)[:, None] * inv[None, :]
    cos = jnp.cos(ang)[None, :, None, :]
    sin = jnp.sin(ang)[None, :, None, :]
    xf = x.astype(jnp.float32)
    x1, x2 = xf[..., :half], xf[..., half:]
    return jnp.concatenate([x1 * cos - x2 * sin, x1 * sin + x2 * cos], axis=-1).astype(x.dtype)

def swiglu(x, w_in, w_out):
    g, u = jnp.split(x @ w_in, 2, axis=-1)
    return (jax.nn.silu(g) * u) @ w_out

def masked_softmax(s, mask):
    s = jnp.where(mask, s, -jnp.inf)
    m = jnp.max(s, axis=-1, keepdims=True)
    m = jnp.where(jnp.isfinite(m), m, 0.0)
    p = jnp.exp(s - m)
    return p / jnp.maximum(jnp.sum(p, axis=-1, keepdims=True), 1e-30)

def _ada(mod, s):
    return mod[:, s, 0][:, None, :], mod[:, s, 1][:, None, :], 1.0 + mod[:, s, 2][:, None, :]

def banded_causal_attention(q, k, v, n_back):
    n, h, l, hd = q.shape
    nb = -(-l // Q_BLOCK)
    lp = nb * Q_BLOCK
    front = (-(-n_back // Q_BLOCK)) * Q_BLOCK
    kw = front + Q_BLOCK
    qp = jnp.pad(q, ((0, 0), (0, 0), (0, lp - l), (0, 0)))
    kp = jnp.pad(k, ((0, 0), (0, 0), (front, lp - l), (0, 0)))
    vp = jnp.pad(v, ((0, 0), (0, 0), (front, lp - l), (0, 0)))
    qi = jnp.arange(Q_BLOCK)[:, None]
    ki = jnp.arange(kw)[None, :]
    dist = front + qi - ki
    band = (dist >= 0) & (dist <= n_back)
    scale = HEAD_DIM ** -0.5

    def step(bi):
        start = bi * Q_BLOCK
        qb = lax.dynamic_slice_in_dim(qp, start, Q_BLOCK, axis=2)
        kb = lax.dynamic_slice_in_dim(kp, start, kw, axis=2)
        vb = lax.dynamic_slice_in_dim(vp, start, kw, axis=2)
        s = jnp.einsum('nhqd,nhkd->nhqk', qb, kb).astype(jnp.float32) * scale
        s = jnp.where(band & (start - front + ki >= 0), s, -jnp.inf)
        m = jnp.max(s, axis=-1, keepdims=True)
        p = jnp.exp(s - m)
        den = jnp.sum(p, axis=-1, keepdims=True)
        o = jnp.einsum('nhqk,nhkd->nhqd', (p / den).astype(vb.dtype), vb)
        return o, (m + jnp.log(den))[..., 0]

    o, lse = lax.map(step, jnp.arange(nb))
    o = jnp.moveaxis(o, 0, 2).reshape(n, h, lp, hd)[:, :, :l]
    lse = jnp.moveaxis(lse, 0, 2).reshape(n, h, lp)[:, :, :l]
    return o, lse

def dilated_attention(q, k, v, window, rate):
    b, s, h, hd = q.shape
    l = s // rate

    def to_res(t):
        return t.reshape(b, l, rate, h, hd).transpose(0, 2, 3, 1, 4).reshape(b * rate, h, l, hd)

    o, lse = banded_causal_attention(to_res(q), to_res(k), to_res(v), window // rate)
    o = o.reshape(b, rate, h, l, hd).transpose(0, 3, 1, 2, 4).reshape(b, s, h, hd)
    lse = lse.reshape(b, rate, h, l).transpose(0, 3, 1, 2).reshape(b, s, h)
    return o, lse

def dilated_mixer(u, w_qkv, q_gain, k_gain, w_o):
    b, s, _ = u.shape
    qkv = (u @ w_qkv).reshape(b, s, N_DIL, 3, N_HEADS, HEAD_DIM)
    outs, lses = [], []
    for g in range(N_DIL):
        q = rope(rms_norm(qkv[:, :, g, 0], q_gain[g]))
        k = rope(rms_norm(qkv[:, :, g, 1], k_gain[g]))
        o, lse = dilated_attention(q, k, qkv[:, :, g, 2], DIL_WINDOWS[g], DIL_RATES[g])
        outs.append(o.astype(jnp.float32))
        lses.append(lse)
    w = jax.nn.softmax(jnp.stack(lses, axis=0), axis=0)
    o = jnp.sum(w[..., None] * jnp.stack(outs, axis=0), axis=0).astype(u.dtype)
    return o.reshape(b, s, N_HEADS * HEAD_DIM) @ w_o

def shared_kv(h, shift, scale, kv_norm_g, w_kv, kv_k_gain, cmp_pos, phi_w1, phi_w2):
    b, s, _ = h.shape
    u = modulate(rms_norm(h, kv_norm_g), shift, scale)
    kv = (u @ w_kv).reshape(b, s, 3, 2, N_KV_HEADS, HEAD_DIM)
    nsb = s // CMP_STRIDE
    nper = CMP_LEN // CMP_STRIDE
    n_c = nsb - nper + 1

    def compress(t, i):
        tb = t.reshape(b, nsb, CMP_STRIDE, N_KV_HEADS, HEAD_DIM)
        blocks = jnp.concatenate([tb[:, j:j + n_c] for j in range(nper)], axis=2)
        blocks = blocks + cmp_pos[i][None, None, :, None, :]
        flat = blocks.transpose(0, 1, 3, 2, 4).reshape(b, n_c, N_KV_HEADS, CMP_LEN * HEAD_DIM)
        return jax.nn.silu(flat @ phi_w1[i]) @ phi_w2[i]

    k_cmp = rms_norm(compress(kv[:, :, 0, 0], 0), kv_k_gain[0]).transpose(0, 2, 1, 3)
    v_cmp = compress(kv[:, :, 0, 1], 1).transpose(0, 2, 1, 3)
    n_s = s // SEL_BLOCK

    def to_blocks(t):
        return t.reshape(b, n_s, SEL_BLOCK, N_KV_HEADS, HEAD_DIM).transpose(0, 3, 1, 2, 4)

    k_slc = to_blocks(rope(rms_norm(kv[:, :, 1, 0], kv_k_gain[1])))
    v_slc = to_blocks(kv[:, :, 1, 1])
    pad = ((0, 0), (0, 0), (SLIDE_WINDOW, 0), (0, 0))
    k_win = jnp.pad(rope(rms_norm(kv[:, :, 2, 0], kv_k_gain[2])).transpose(0, 2, 1, 3), pad)
    v_win = jnp.pad(kv[:, :, 2, 1].transpose(0, 2, 1, 3), pad)
    return k_cmp, v_cmp, k_slc, v_slc, k_win, v_win

def block_importance(p, n_s):
    r = SEL_BLOCK // CMP_STRIDE
    nper = CMP_LEN // CMP_STRIDE
    left = nper - 1
    n_c = p.shape[-1]
    right = r * n_s + r - n_c
    pp = jnp.pad(p, [(0, 0)] * (p.ndim - 1) + [(left, right)])
    imp = None
    for o in range(-left, r):
        w = sum(1 for m in range(r) for n in range(nper) if m - n == o)
        sl = pp[..., o + left:o + left + r * n_s:r]
        imp = w * sl if imp is None else imp + w * sl
    return imp

def nsa_mixer(u, k_cmp, v_cmp, k_slc, v_slc, k_win, v_win, w_qg, q_gain, w_o):
    b, s, _ = u.shape
    grp = N_HEADS // N_KV_HEADS
    hdim = N_HEADS * HEAD_DIM
    qg = u @ w_qg
    q = rms_norm(qg[..., :hdim].reshape(b, s, N_HEADS, HEAD_DIM), q_gain)
    gates = jax.nn.sigmoid(qg[..., hdim:].astype(jnp.float32))
    gates = gates.reshape(b, s, 3, N_KV_HEADS, grp).transpose(2, 0, 3, 4, 1)

    def to_grp(t):
        return t.reshape(b, s, N_KV_HEADS, grp, HEAD_DIM).transpose(0, 2, 3, 1, 4)

    q_nope = to_grp(q)
    q_rope = to_grp(rope(q))
    n_c = k_cmp.shape[2]
    n_s = k_slc.shape[2]
    topk = min(N_SELECT, n_s)
    cmp_end = jnp.arange(n_c) * CMP_STRIDE + CMP_LEN - 1
    blk = jnp.arange(n_s)
    qi = jnp.arange(Q_BLOCK)
    ki = jnp.arange(SLIDE_WINDOW + Q_BLOCK)[None, :]
    wdist = SLIDE_WINDOW + qi[:, None] - ki
    wband = (wdist >= 0) & (wdist < SLIDE_WINDOW)
    bi_idx = jnp.arange(b)[:, None, None, None]
    hi_idx = jnp.arange(N_KV_HEADS)[None, :, None, None]
    scale = HEAD_DIM ** -0.5

    def step(bi):
        start = bi * Q_BLOCK
        t = start + qi
        qn = lax.dynamic_slice_in_dim(q_nope, start, Q_BLOCK, axis=3)
        qr = lax.dynamic_slice_in_dim(q_rope, start, Q_BLOCK, axis=3)
        gb = lax.dynamic_slice_in_dim(gates, start, Q_BLOCK, axis=4)
        sc = jnp.einsum('bkgqd,bkcd->bkgqc', qn, k_cmp).astype(jnp.float32) * scale
        p_cmp = masked_softmax(sc, cmp_end[None, :] <= t[:, None])
        o_cmp = jnp.einsum('bkgqc,bkcd->bkgqd', p_cmp.astype(v_cmp.dtype), v_cmp)
        imp = block_importance(jnp.sum(p_cmp, axis=2), n_s)
        jt = (t // SEL_BLOCK)[:, None]
        forced = (blk == 0) | (blk == jt) | (blk == jt - 1)
        imp = jnp.where(blk > jt, -jnp.inf, jnp.where(forced, jnp.inf, imp))
        _, idx = lax.top_k(imp, topk)
        ks = k_slc[bi_idx, hi_idx, idx].reshape(b, N_KV_HEADS, Q_BLOCK, topk * SEL_BLOCK, HEAD_DIM)
        vs = v_slc[bi_idx, hi_idx, idx].reshape(b, N_KV_HEADS, Q_BLOCK, topk * SEL_BLOCK, HEAD_DIM)
        kpos = (idx[..., None] * SEL_BLOCK + jnp.arange(SEL_BLOCK)).reshape(b, N_KV_HEADS, Q_BLOCK, topk * SEL_BLOCK)
        ss = jnp.einsum('bkgqd,bkqnd->bkgqn', qr, ks).astype(jnp.float32) * scale
        p_s = masked_softmax(ss, (kpos <= t[:, None])[:, :, None])
        o_slc = jnp.einsum('bkgqn,bkqnd->bkgqd', p_s.astype(vs.dtype), vs)
        kw = lax.dynamic_slice_in_dim(k_win, start, SLIDE_WINDOW + Q_BLOCK, axis=2)
        vw = lax.dynamic_slice_in_dim(v_win, start, SLIDE_WINDOW + Q_BLOCK, axis=2)
        sw = jnp.einsum('bkgqd,bknd->bkgqn', qr, kw).astype(jnp.float32) * scale
        p_w = masked_softmax(sw, wband & (start - SLIDE_WINDOW + ki >= 0))
        o_win = jnp.einsum('bkgqn,bknd->bkgqd', p_w.astype(vw.dtype), vw)
        o = gb[0][..., None] * o_cmp + gb[1][..., None] * o_slc + gb[2][..., None] * o_win
        return o.astype(u.dtype)

    o = lax.map(step, jnp.arange(s // Q_BLOCK))
    o = o.transpose(1, 0, 4, 2, 3, 5).reshape(b, s, hdim)
    return o @ w_o

def second_inputs(seed: int = 0) -> dict:
    key = jax.random.key(seed)
    ks = jax.random.split(key, 22)
    n_a = DEPTH_2 // 2
    n_b = DEPTH_2 - n_a
    d = D_MODEL
    hdim = N_HEADS * HEAD_DIM

    def nrm(k, shape, fan_in, gain=1.0):
        return jax.random.normal(k, shape, jnp.float32) * (gain * fan_in ** -0.5)

    def gain_init(k, shape):
        return 1.0 + 0.02 * jax.random.normal(k, shape, jnp.float32)

    return {
        'x': jax.random.normal(ks[0], (BATCH, SEQ, d), jnp.float32),
        'c': jax.random.normal(ks[1], (BATCH, d), jnp.float32),
        'norm_g': gain_init(ks[2], (DEPTH_2, 3, d)),
        'w_ada': nrm(ks[3], (DEPTH_2, d, 9 * d), d, 0.1),
        'b_ada': 0.01 * jax.random.normal(ks[4], (DEPTH_2, 9 * d), jnp.float32),
        'ffn_w_in': nrm(ks[5], (DEPTH_2, 2, d, 2 * D_FF_2), d),
        'ffn_w_out': nrm(ks[6], (DEPTH_2, 2, D_FF_2, d), D_FF_2),
        'a_w_qkv': nrm(ks[7], (n_a, d, N_DIL * 3 * hdim), d),
        'a_q_gain': gain_init(ks[8], (n_a, N_DIL, HEAD_DIM)),
        'a_k_gain': gain_init(ks[9], (n_a, N_DIL, HEAD_DIM)),
        'a_w_o': nrm(ks[10], (n_a, hdim, d), hdim),
        'kv_norm_g': gain_init(ks[11], (d,)),
        'w_ada_kv': nrm(ks[12], (d, 2 * d), d, 0.1),
        'b_ada_kv': 0.01 * jax.random.normal(ks[13], (2 * d,), jnp.float32),
        'w_kv': nrm(ks[14], (d, 3 * 2 * N_KV_HEADS * HEAD_DIM), d),
        'kv_k_gain': gain_init(ks[15], (3, HEAD_DIM)),
        'cmp_pos': 0.1 * jax.random.normal(ks[16], (2, CMP_LEN, HEAD_DIM), jnp.float32),
        'phi_w1': nrm(ks[17], (2, CMP_LEN * HEAD_DIM, CMP_HIDDEN), CMP_LEN * HEAD_DIM),
        'phi_w2': nrm(ks[18], (2, CMP_HIDDEN, HEAD_DIM), CMP_HIDDEN),
        'b_w_qg': nrm(ks[19], (n_b, d, hdim + 3 * N_HEADS), d),
        'b_q_gain': gain_init(ks[20], (n_b, HEAD_DIM)),
        'b_w_o': nrm(ks[21], (n_b, hdim, d), hdim),
    }

def second_block(x, c, norm_g, w_ada, b_ada, ffn_w_in, ffn_w_out, a_w_qkv, a_q_gain, a_k_gain, a_w_o,
              kv_norm_g, w_ada_kv, b_ada_kv, w_kv, kv_k_gain, cmp_pos, phi_w1, phi_w2,
              b_w_qg, b_q_gain, b_w_o):
    n_a = DEPTH_2 // 2
    bsz = x.shape[0]
    c_act = jax.nn.silu(c)
    h = x
    shared = None
    for l in range(DEPTH_2):
        mod = (c_act @ w_ada[l] + b_ada[l]).reshape(bsz, 3, 3, D_MODEL)
        sh, sc, gt = _ada(mod, 0)
        h = h + 0.5 * gt * swiglu(modulate(rms_norm(h, norm_g[l, 0]), sh, sc), ffn_w_in[l, 0], ffn_w_out[l, 0])
        sh, sc, gt = _ada(mod, 1)
        u = modulate(rms_norm(h, norm_g[l, 1]), sh, sc)
        if l < n_a:
            y = dilated_mixer(u, a_w_qkv[l], a_q_gain[l], a_k_gain[l], a_w_o[l])
        else:
            j = l - n_a
            y = nsa_mixer(u, *shared, b_w_qg[j], b_q_gain[j], b_w_o[j])
        h = h + gt * y
        sh, sc, gt = _ada(mod, 2)
        h = h + 0.5 * gt * swiglu(modulate(rms_norm(h, norm_g[l, 2]), sh, sc), ffn_w_in[l, 1], ffn_w_out[l, 1])
        if l == n_a - 1:
            kv_mod = (c_act @ w_ada_kv + b_ada_kv).reshape(bsz, 2, D_MODEL)
            shared = shared_kv(h, kv_mod[:, 0][:, None, :], kv_mod[:, 1][:, None, :], kv_norm_g, w_kv,
                               kv_k_gain, cmp_pos, phi_w1, phi_w2)
    return h


def setup_inputs(seed=0):
    out = dict(first_inputs(seed))
    for name, value in second_inputs(seed + 1).items():
        if name != "x":
            out[name + "_2"] = value
    return out


def reference(
    x, mem, positions, g_mix_pre, w_in, conv_w, a_log, dt_bias, g_dn_out, attn_sink, w_out,
    g_mix_post, g_cross_pre, g_mem, w_cq, w_ckv, w_co, g_cross_post, g_ffn_pre, w_gate_up,
    w_down, g_ffn_post, c_2, norm_g_2, w_ada_2, b_ada_2, ffn_w_in_2, ffn_w_out_2, a_w_qkv_2,
    a_q_gain_2, a_k_gain_2, a_w_o_2, kv_norm_g_2, w_ada_kv_2, b_ada_kv_2, w_kv_2, kv_k_gain_2,
    cmp_pos_2, phi_w1_2, phi_w2_2, b_w_qg_2, b_q_gain_2, b_w_o_2,
):
    x = first_block(
        x, mem, positions, g_mix_pre, w_in, conv_w, a_log, dt_bias, g_dn_out, attn_sink, w_out,
        g_mix_post, g_cross_pre, g_mem, w_cq, w_ckv, w_co, g_cross_post, g_ffn_pre, w_gate_up,
        w_down, g_ffn_post,
    )
    return second_block(
        x, c_2, norm_g_2, w_ada_2, b_ada_2, ffn_w_in_2, ffn_w_out_2, a_w_qkv_2, a_q_gain_2,
        a_k_gain_2, a_w_o_2, kv_norm_g_2, w_ada_kv_2, b_ada_kv_2, w_kv_2, kv_k_gain_2,
        cmp_pos_2, phi_w1_2, phi_w2_2, b_w_qg_2, b_q_gain_2, b_w_o_2,
    )


_drawn_inputs = setup_inputs


def setup_inputs(seed=0):
    import zlib

    import numpy as np

    out = dict(_drawn_inputs(seed))
    spreads = {}
    factors = {'g_dn_out': 3.571,
     'attn_sink': 8.0,
     'g_mix_post': 3.401,
     'g_cross_pre': 4.378,
     'g_mem': 2.767,
     'g_cross_post': 4.084,
     'g_ffn_pre': 3.833,
     'g_ffn_post': 5.255,
     'norm_g_2': 6.024,
     'b_ada_2': 6.771,
     'a_q_gain_2': 8.0,
     'a_k_gain_2': 8.0,
     'kv_norm_g_2': 8.0,
     'b_ada_kv_2': 8.0,
     'kv_k_gain_2': 8.0,
     'cmp_pos_2': 4.33,
     'b_q_gain_2': 8.0}
    for name, (base, spread) in spreads.items():
        noise = np.random.default_rng([zlib.crc32(name.encode()), seed]).standard_normal(out[name].shape)
        drawn = base * np.exp(spread * noise) if base else spread * noise
        out[name] = __import__('jax').numpy.asarray(drawn.astype(out[name].dtype))
    for name, factor in factors.items():
        out[name] = (out[name] * factor).astype(out[name].dtype)
    return out
```

```python
from contextlib import ExitStack, contextmanager

import numpy as np

import concourse.bass as bass
from concourse import mybir

F32 = mybir.dt.float32
I32 = mybir.dt.int32
ALU = mybir.AluOpType
ACT = mybir.ActivationFunctionType
AX_X = mybir.AxisListType.X

P = 128
D = 1024
KT = D // P
S = 512
NB = S // P
MEM = 256
EPS = 1e-6
FF = 2816
FT = FF // P
HALF = 64
NEG = -1e30
FLOOR = -1e29
LOWEST = -3e38
SLAB = 4096

AH, AKV = 8, 2
DH = 4
XH = 4
CONV = 5
H2 = 16
PAIRS = H2 // 2
NCMP = S // 16 - 1
LEVELS = 7

STREAM = [
    ("ada", 40, 4096),
    ("w_in", 6, 4096),
    ("w_out", 2, 4096),
    ("w_ckv", 4, 4096),
    ("w_cq", 2, 4096),
    ("w_co", 2, 4096),
    ("up_0", 11, 4096), ("down_0", 8, FF),
    ("up_1", 11, 4096), ("down_1", 8, FF),
    ("qkv", 3 * PAIRS, 3072),
    ("a_w_o", 2, 4096),
    ("up_2", 11, 4096), ("down_2", 8, FF),
    ("w_kv", 2, 4096),
    ("phi", 2, 4096),
    ("phi2", 1, 256),
    ("up_3", 11, 4096), ("down_3", 8, FF),
    ("gates", 1, 512),
    ("w_q", 2, 4096),
    ("b_w_o", 2, 4096),
    ("up_4", 11, 4096), ("down_4", 8, FF),
]


def layout(sizes):
    at, out = 0, {}
    for name, n in sizes:
        out[name] = (at, n)
        at += n
    return out, at


CONST, N_CONST = layout([
    ("ident", P), ("ones", P), ("swap", P), ("head2", 2), ("tri_f", P), ("tri_b", P),
    ("levels", 2 * LEVELS * P), ("win", 3 * P), ("causal", 4 * P), ("dil0", 4 * S), ("dil12", 2 * P),
    ("cmp", NB * 32), ("cos_n", S), ("sin_n", S), ("cos_p", S), ("sin_p", S), ("freq", 1), ("sign", 1),
])

VECS = [
    ("g_mix_pre", 8), ("g_mix_post", 8), ("g_cross_pre", 8), ("g_mem", 8), ("g_cross_post", 8),
    ("g_ffn_pre", 8), ("g_ffn_post", 8), ("g_dn_out", 1), ("conv_w", 12 * CONV),
    ("a_log", 8), ("dt_bias", 8), ("attn_sink", AH),
    ("c_2", 8), ("norm_g_2", 48), ("b_ada", 160), ("kv_norm_g_2", 8),
    ("a_q_gain_2", 3), ("a_k_gain_2", 3), ("kv_k_gain_2", 3), ("b_q_gain_2", 1), ("cmp_pos_2", 64),
]
VEC, N_VEC = layout(VECS)


def constants():
    c = np.zeros((P, N_CONST), np.float32)

    def put(name, a):
        at, n = CONST[name]
        c[:, at:at + n] = np.asarray(a, np.float32).reshape(P, n)

    i, j = np.arange(P)[:, None], np.arange(P)[None, :]
    put("ident", i == j)
    put("ones", np.ones((P, P)))
    put("swap", (i // 64 == j // 64) & ((i % 64 + 32) % 64 == j % 64))
    put("head2", i // 64 == np.arange(2)[None, :])
    put("tri_f", i <= j)
    put("tri_b", i >= j)
    levels = np.zeros((P, 2, LEVELS, P))
    for n in range(LEVELS):
        b = 1 << n
        levels[:, 0, n] = ((j // b) % 2 == 1) & (i // b == j // b - 1)
        levels[:, 1, n] = ((i // b) % 2 == 1) & (j // b == i // b - 1)
    put("levels", levels)
    k = np.arange(3 * P)[None, :]
    put("win", np.where(np.abs(k - P - i) <= P, 0, NEG))
    put("causal", np.concatenate([np.zeros((P, 3 * P)), np.where(j <= i, 0, NEG)], 1))
    at = np.arange(S)
    token = 4 * (at % P) + at // P
    dil0 = np.zeros((P, 4, S))
    for r in range(4):
        back = (4 * np.arange(P) + r)[:, None] - token[None, :]
        dil0[:, r] = np.where((back >= 0) & (back <= P), 0, NEG)
    put("dil0", dil0)
    put("dil12", np.concatenate([np.where(j <= i, 0, NEG), np.where((j <= i) & ((i - j) % 4 == 0), 0, NEG)], 1))
    q = np.arange(P)[:, None, None] + P * np.arange(NB)[None, :, None]
    put("cmp", np.where(16 * np.arange(32)[None, None, :] + 31 <= q, 0, NEG))
    inv = (np.float32(10000.0) ** (-np.arange(32, dtype=np.float32) / np.float32(32))).astype(np.float32)
    inv = inv[np.arange(P) % 32]
    sign = np.where(np.arange(P) % 64 < 32, -1.0, 1.0)
    ang = (np.arange(S, dtype=np.float32)[None, :] * inv[:, None]).astype(np.float64)
    put("cos_n", np.cos(ang))
    put("sin_n", np.sin(ang) * sign[:, None])
    put("cos_p", np.cos(ang)[:, token])
    put("sin_p", (np.sin(ang) * sign[:, None])[:, token])
    put("freq", inv)
    put("sign", sign)
    return c


def slabs_of(w, cols=512):
    k, n = w.shape
    t = w.reshape(k // P, P, n // cols, cols).transpose(2, 1, 0, 3)
    return t.reshape(n // cols, P, -1)


def weight_stream(x):
    def up(w):
        g, u = w[:, :FF].reshape(D, FT, P), w[:, FF:].reshape(D, FT, P)
        return slabs_of(np.stack([g, u], 2).reshape(D, 2 * FF))

    def twice(w):
        return [w[:, 0:64], w[:, 0:64], w[:, 64:128], w[:, 64:128]]

    w_in = x["w_in"][0]
    w_in = np.concatenate(
        [w_in[:, 0:512]] + twice(w_in[:, 512:640]) + [w_in[:, 768:2304], w_in[:, 2304:2816], w_in[:, 640:768],
         w_in[:, 2816:2832], np.zeros((D, 112), np.float32)], 1)
    qkv = x["a_w_qkv_2"][0].reshape(D, 3, 3, PAIRS, P).transpose(0, 3, 1, 2, 4).reshape(D, -1)
    w_kv = x["w_kv_2"].reshape(D, 3, 2, P)
    w_kv = np.concatenate([w_kv[:, 0, 0], w_kv[:, 0, 1]] + twice(w_kv[:, 1, 0]) + twice(w_kv[:, 2, 0])
                          + [w_kv[:, 1, 1], w_kv[:, 2, 1]], 1)
    phi1 = x["phi_w1_2"].reshape(2, 32, 64, P).transpose(2, 0, 1, 3).reshape(64, 2 * SLAB)
    phi1 = np.concatenate([phi1, phi1], 0).reshape(P, 2, SLAB).transpose(1, 0, 2)
    phi2 = x["phi_w2_2"].transpose(1, 0, 2).reshape(P, 128)
    phi2 = np.concatenate([phi2[:, 0:64], phi2[:, 0:64], phi2[:, 64:128], phi2[:, 64:128]], 1)
    qg = x["b_w_qg_2"][0]
    gates = np.concatenate([qg[:, 1024:], np.zeros((D, 16), np.float32)], 1)
    ffn_in, ffn_out = x["ffn_w_in_2"], x["ffn_w_out_2"]
    parts = {
        "ada": np.concatenate([slabs_of(w) for w in (x["w_ada_2"][0], x["w_ada_2"][1], x["w_ada_kv_2"])]),
        "w_in": slabs_of(w_in), "w_out": slabs_of(x["w_out"][0]), "w_ckv": slabs_of(x["w_ckv"][0]),
        "w_cq": slabs_of(x["w_cq"][0]), "w_co": slabs_of(x["w_co"][0]),
        "up_0": up(x["w_gate_up"][0]), "down_0": slabs_of(x["w_down"][0], P),
        "qkv": slabs_of(qkv, 3 * P), "a_w_o": slabs_of(x["a_w_o_2"][0]),
        "w_kv": slabs_of(w_kv), "phi": phi1, "phi2": phi2[None],
        "gates": slabs_of(gates, 64), "w_q": slabs_of(qg[:, :1024]), "b_w_o": slabs_of(x["b_w_o_2"][0]),
    }
    for n in range(4):
        parts[f"up_{n + 1}"] = up(ffn_in[n // 2, n % 2])
        parts[f"down_{n + 1}"] = slabs_of(ffn_out[n // 2, n % 2], P)
    out = np.zeros((sum(n for _, n, _ in STREAM), P, SLAB), np.float32)
    at = 0
    for name, n, cols in STREAM:
        assert parts[name].shape == (n, P, cols), (name, parts[name].shape)
        out[at:at + n, :, :cols] = parts[name]
        at += n
    return out


def vectors(x):
    def cols(a):
        return np.asarray(a).reshape(-1, P).T

    def rows(a):
        return np.broadcast_to(np.asarray(a).reshape(1, -1), (P, a.size))

    def heads(a):
        a = np.asarray(a).reshape(-1, HALF).T
        return np.concatenate([a, a], 0)

    parts = {n: cols(x[n]) for n in ("g_mix_pre", "g_mix_post", "g_cross_pre", "g_mem", "g_cross_post",
                                     "g_ffn_pre", "g_ffn_post", "g_dn_out", "c_2", "norm_g_2", "kv_norm_g_2")}
    parts |= {n: rows(x[n]) for n in ("a_log", "dt_bias", "attn_sink")}
    parts |= {n: heads(x[n]) for n in ("a_q_gain_2", "a_k_gain_2", "kv_k_gain_2", "b_q_gain_2", "cmp_pos_2")}
    parts["conv_w"] = x["conv_w"][0].reshape(CONV, 12, P).transpose(2, 1, 0).reshape(P, -1)
    parts["b_ada"] = np.concatenate([cols(x["b_ada_2"]), cols(x["b_ada_kv_2"])], 1)
    return np.ascontiguousarray(np.concatenate([parts[n] for n, _ in VECS], 1))


class Seat:

    def __init__(self, n=1):
        self.n, self.pos, self.loop = n, 0, None

    def next(self):
        at, self.pos = self.pos, self.pos + 1
        use = at // self.n
        if self.loop is not None:
            i, per = self.loop
            use = use + i * (per // self.n)
        return at % self.n, use


@contextmanager
def repeat(eng, n, seats):
    starts = [s.pos for s, _ in seats]
    with eng.Fori(0, n) as i:
        for s, per in seats:
            assert per % s.n == 0
            s.loop = (i, per)
        yield i
    for (s, per), start in zip(seats, starts):
        assert s.pos - start == per, (s.pos, start, per)
        s.pos, s.loop = start + n * per, None


class Ring:
    def __init__(self, sem, name, n):
        self.n = n
        self.full = [sem(f"{name}_full{i}") for i in range(n)]
        self.free = [sem(f"{name}_free{i}") for i in range(n)]

    def seat(self):
        return Seat(self.n)


def two_blocks(nc, a, until=None):
    with ExitStack() as ctx:
        def sb(name, shape, dt=F32):
            return ctx.enter_context(nc.sbuf_tensor(f"{name}_sb", shape, dt))

        def sem(name):
            return ctx.enter_context(nc.semaphore(name))

        h = sb("h", [P, KT, S])
        xn = sb("xn", [P, KT, S])
        y = sb("y", [P, KT, S])
        sq = sb("sq", [P, KT, S])
        slab = [sb(f"slab{i}", [P, SLAB]) for i in range(2)]
        const = sb("const", [P, N_CONST])
        vec = sb("vec", [P, N_VEC])
        mod = sb("mod", [P, 160])
        fold = sb("fold", [P, 7, 3, KT])
        small = sb("small", [P, 256])
        keep = sb("keep", [P, 3456])
        work = sb("work", [P, 15616])
        bank = [ctx.enter_context(nc.psum_tensor(f"bank{i}", [P, S], F32)) for i in range(8)]

        def K(name, *shape):
            at, n = CONST[name]
            v = const[:, at:at + n]
            if len(shape) == 2:
                return v.rearrange("p (a b) -> p a b", a=shape[0])
            if len(shape) == 3:
                return v.rearrange("p (a b c) -> p a b c", a=shape[0], b=shape[1])
            return v

        def V(name, i=0, n=None):
            at, size = VEC[name]
            return vec[:, at + i:at + (size if n is None else i + n)]

        def cut(t, at, *shape):
            n = int(np.prod(shape))
            v = t[:, at:at + n]
            if len(shape) == 2:
                return v.rearrange("p (a b) -> p a b", a=shape[0])
            if len(shape) == 3:
                return v.rearrange("p (a b c) -> p a b c", a=shape[0], b=shape[1])
            return v

        ident, ones1 = K("ident"), K("ones")[:, 0:1]

        acc = Ring(sem, "acc", 4)
        sc = Ring(sem, "scores", 2)
        tp = Ring(sem, "turned", 2)
        cvr = Ring(sem, "conv_in", 2)
        sgr = Ring(sem, "silu_gate", 2)
        score_bank, turn_bank = bank[4:6], bank[6:8]
        slab_loaded = [sem(f"slab_loaded{i}") for i in range(2)]
        slab_used = [sem(f"slab_used{i}") for i in range(2)]
        inputs_loaded = sem("inputs_loaded")
        out_stored = sem("out_stored")
        squared = sem("squared")
        rooted = sem("rooted")
        inverted = sem("inverted")
        maxed = sem("maxed")
        exped = sem("exped")
        weighed = sem("weighed")
        copied = sem("copied")
        pv_done = sem("pv_done")
        normed = sem("normed")
        heads_ready = sem("heads_ready")
        angles_ready = sem("angles_ready")
        hidden_ready = sem("hidden_ready")
        mem_loaded = sem("mem_loaded")
        dve_step = sem("dve_step")
        act_step = sem("act_step")
        gated = sem("gated")
        done = {e: sem(f"stage_done_{e}") for e in ("pe", "act", "dve", "pool")}

        counted = {"squared": squared, "rooted": rooted, "inverted": inverted, "maxed": maxed, "exped": exped,
                   "weighed": weighed, "copied": copied, "pv_done": pv_done, "normed": normed,
                   "heads_ready": heads_ready, "dve_step": dve_step, "act_step": act_step}

        class Stop(Exception):
            pass

        places = []

        class Engine:

            def __init__(self, name, eng):
                self.name, self.eng, self.stages = name, eng, 0
                self.acc, self.sc, self.tp = acc.seat(), sc.seat(), tp.seat()
                self.slab, self.cv, self.sg = Seat(2), cvr.seat(), sgr.seat()
                self.seats = {}

            def seat(self, s):
                return self.seats.setdefault(id(s), Seat())

            def nth(self, s):
                return self.seat(s).next()[1] + 1

            def rates(self, slab=None, acc=None, sc=None, tp=None, **counts):
                named = [(self.slab, slab), (self.acc, acc), (self.sc, sc), (self.tp, tp)]
                named += [(self.seat(counted[n]), per) for n, per in counts.items()]
                return [(s, per) for s, per in named if per]

            def link(self, ins, s):
                ins.then_inc(s, 1)
                self.eng.wait_ge(s, self.nth(s))

            def stage_end(self, name):
                self.stages += 1
                self.eng.drain().then_inc(done[self.name], 1)
                for other, s in done.items():
                    if other != self.name:
                        self.eng.wait_ge(s, self.stages)
                if self.name == "pe":
                    places.append((name, self.acc.pos, self.sc.pos, self.tp.pos))
                else:
                    what, self.acc.pos, self.sc.pos, self.tp.pos = places[self.stages - 1]
                    assert what == name, (what, name)
                if name == until:
                    raise Stop

            def take(self, ring, seat):
                i, use = seat.next()
                self.eng.wait_ge(ring.full[i], use + 1)
                return i

            def give(self, ring, seat):
                i, use = seat.next()
                self.eng.wait_ge(ring.free[i], use + 1)
                return i

        block = ctx.enter_context(nc.Block())

        b1_qkv = cut(work, 0, 12, S)
        b1_vtm = cut(work, 6144, NB, 144)
        b1_cv = [cut(work, 6720, S + 4), cut(work, 6720 + 516, S + 4)]
        b1_gate = cut(keep, 0, 4, S)
        b1_tmp = cut(work, 7760, 4, S)
        b1_cos, b1_sin = b1_tmp[:, 0, :], b1_tmp[:, 1, :]
        S_SB = [cut(work, 9856, 768), cut(work, 10624, 768)]
        PR = [cut(work, 11392, 768), cut(work, 12160, 768)]
        PT = [cut(work, 12928, 1024), cut(work, 13952, 1024)]
        pt_bank = [[cut(PT_, 0, S), cut(PT_, S, S)] for PT_ in PT]

        m_col = [small[:, 0:2], small[:, 2:4]]
        neg_m = [small[:, 4:5], small[:, 5:6]]
        den = [small[:, 6:7], small[:, 7:8]]
        sink_e = [small[:, 8:9], small[:, 9:10]]
        inv_den = [small[:, 10:11], small[:, 11:12]]
        root = small[:, 16:64]
        inv = small[:, 64:112]
        cact = small[:, 112:120]
        gates = cut(keep, 3072, NB, 48)

        class Unit:

            def __init__(self, scores, masks, values, least=LOWEST, sink=None, floor=False, gate=None,
                         opens=False, closes=False):
                self.scores, self.masks, self.values = scores, masks, values
                self.least, self.sink, self.floor, self.gate = least, sink, floor, gate
                self.opens, self.closes = opens, closes
                self.n = sum(n for _, n in scores)
                self.nb = len(scores)
                chunks = {}
                for col, keys, *_ in values:
                    chunks[col] = keys
                self.chunks = sorted(chunks.items())

        def attend(e, units, out_banks, finish):
            eng = e.eng
            outs = {}
            n = len(units)
            for i in range(n + 2):
                par = i % 2
                if e.name == "pe":
                    if i < n:
                        for parts, _ in units[i].scores:
                            s = e.give(sc, e.sc)
                            for at, cols, prods in parts:
                                for x, (lhsT, rhs) in enumerate(prods):
                                    mm = eng.matmul(score_bank[s][:, at:at + cols], lhsT, rhs, start=x == 0,
                                                    stop=x == len(prods) - 1)
                            mm.then_inc(sc.full[s], 1)
                    if 1 <= i <= n:
                        u = units[i - 1]
                        eng.wait_ge(weighed, e.nth(weighed))
                        for b in range(u.nb):
                            t = e.give(tp, e.tp)
                            mine = [(c, k) for c, k in u.chunks if c // S == b] if u.nb > 1 else u.chunks
                            for x, (col, keys) in enumerate(mine):
                                mm = eng.transpose(turn_bank[t][0:keys, x * P:(x + 1) * P],
                                                   PR[1 - par][:, col:col + keys], ident)
                            mm.then_inc(tp.full[t], 1)
                    if i >= 2:
                        u = units[i - 2]
                        eng.wait_ge(copied, e.nth(copied))
                        if u.opens:
                            outs.clear()
                            for o in range(out_banks):
                                outs[o] = e.give(acc, e.acc)
                        where = {c: x for x, (c, _) in enumerate(u.chunks)}
                        for col, keys, lhsT, (o, r0, r1, c0), first, last in u.values:
                            x = where[col]
                            mm = eng.matmul(bank[outs[o]][r0:r1, c0:c0 + P], lhsT,
                                            PT[par][0:keys, x * P:(x + 1) * P], start=first, stop=last)
                        mm.then_inc(pv_done, 1)
                        if u.closes:
                            for o in range(out_banks):
                                eng.drain().then_inc(acc.full[outs[o]], 1)
                elif e.name == "dve":
                    if i < n:
                        u = units[i]
                        col = 0
                        for b, ((_, cols), mask) in enumerate(zip(u.scores, u.masks)):
                            s = e.take(sc, e.sc)
                            if e.sc.loop is not None:
                                eng.memset(small[:, 124 + b:125 + b], 0.0)
                            eng.tensor_tensor_reduce(
                                out=S_SB[par][:, col:col + cols], in0=score_bank[s][:, 0:cols], in1=mask,
                                scale=1.0, scalar=u.least, op0=ALU.add, op1=ALU.max,
                                accum_out=m_col[par][:, b:b + 1]).then_inc(sc.free[s], 1)
                            col += cols
                        eng.drain()
                        if u.nb == 2:
                            e.link(eng.tensor_tensor(m_col[par][:, 0:1], m_col[par][:, 0:1], m_col[par][:, 1:2],
                                                     ALU.max), dve_step)
                        if u.sink is not None:
                            e.link(eng.tensor_tensor(m_col[par][:, 0:1], m_col[par][:, 0:1], u.sink, ALU.max), dve_step)
                        eng.tensor_scalar(neg_m[par], m_col[par][:, 0:1], -1.0, None, ALU.mult).then_inc(maxed, 1)
                    if 1 <= i <= n:
                        u, q = units[i - 1], 1 - par
                        eng.wait_ge(exped, e.nth(exped))
                        if u.sink is not None:
                            e.link(eng.tensor_tensor(den[q], den[q], sink_e[q], ALU.add), dve_step)
                        if u.floor:
                            e.link(eng.tensor_scalar(den[q], den[q], 1e-30, None, ALU.max), dve_step)
                        e.link(eng.reciprocal(inv_den[q], den[q]), dve_step)
                        if u.gate is not None:
                            eng.tensor_scalar(PR[q][:, 0:u.n], PR[q][:, 0:u.n], inv_den[q], u.gate, ALU.mult,
                                              ALU.mult).then_inc(weighed, 1)
                        else:
                            eng.tensor_scalar(PR[q][:, 0:u.n], PR[q][:, 0:u.n], inv_den[q], None,
                                              ALU.mult).then_inc(weighed, 1)
                elif e.name == "act":
                    if i < n:
                        u = units[i]
                        eng.wait_ge(maxed, e.nth(maxed))
                        if u.sink is not None:
                            eng.activation(sink_e[par], u.sink, ACT.Exp, bias=neg_m[par])
                        eng.activation(PR[par][:, 0:u.n], S_SB[par][:, 0:u.n], ACT.Exp, bias=neg_m[par],
                                       accum_out=den[par]).then_inc(exped, 1)
                    if 1 <= i <= n:
                        u, q = units[i - 1], 1 - par
                        if i >= 3:
                            eng.wait_ge(pv_done, e.nth(pv_done))
                        for b in range(u.nb):
                            t = e.take(tp, e.tp)
                            mine = [(c, k) for c, k in u.chunks if c // S == b] if u.nb > 1 else u.chunks
                            rows = mine[0][1]
                            cp = eng.activation(pt_bank[q][b][0:rows, 0:len(mine) * P],
                                                turn_bank[t][0:rows, 0:len(mine) * P], ACT.Copy)
                            if b == u.nb - 1:
                                cp.then_inc(copied, 1)
                                eng.drain().then_inc(tp.free[t], 1)
                            else:
                                cp.then_inc(tp.free[t], 1)
                    if i >= 2 and units[i - 2].closes:
                        for o in range(out_banks):
                            s = e.take(acc, e.acc)
                            finish(o, bank[s], i - 2).then_inc(acc.free[s], 1)
            if e.name == "act":
                e.seat(pv_done).pos += 1
                eng.wait_ge(pv_done, e.nth(pv_done))

        def pe_cols(e, sqv, tiles, nb, summed, sub):
            pe = e.eng
            pe.wait_ge(squared, e.nth(squared))
            s = e.give(acc, e.acc)
            rhs = ones1 if sub == 1 else K("head2")
            for j in range(1 if summed else tiles):
                for b in range(nb):
                    at = (j * nb + b) * sub
                    inner = range(tiles) if summed else [j]
                    for x in inner:
                        mm = pe.matmul(bank[s][:, at:at + sub], sqv[:, x, b * P:(b + 1) * P], rhs,
                                       start=x == inner[0], stop=x == inner[-1])
            mm.then_inc(acc.full[s], 1)
            pe.wait_ge(inverted, e.nth(inverted))

        def pe_spread(e, nb, sub, j=0):
            pe = e.eng
            s = e.give(acc, e.acc)
            for b in range(nb):
                for x in range(sub):
                    at = (j * nb + b) * sub + x
                    r = P // sub
                    mm = pe.matmul(bank[s][x * r:(x + 1) * r, b * P:(b + 1) * P],
                                   inv[:, at:at + 1].to_broadcast([P, r]), ident, start=True, stop=True)
            mm.then_inc(acc.full[s], 1)

        def pe_pass(e, n):
            for _ in range(n):
                s = e.give(acc, e.acc)
                e.eng.matmul(bank[s][:, 0:1], ident, ones1, start=True, stop=True).then_inc(acc.full[s], 1)

        def pe_norm(e, width=S):
            pe_cols(e, sq, KT, width // P, True, 1)
            pe_spread(e, width // P, 1)

        def pe_slab(e, tiles, nkt, stride, x, width=S, cols=P, more=()):
            pe = e.eng
            i, use = e.slab.next()
            pe.wait_ge(slab_loaded[i], 16 * (use + 1))
            for t in tiles:
                s = e.give(acc, e.acc)
                for k in range(nkt):
                    mm = pe.matmul(bank[s][:, 0:width], slab[i][:, k * stride + t * P:k * stride + t * P + cols],
                                   x(k), start=k == 0, stop=k == nkt - 1)
                mm.then_inc(acc.full[s], 1)
            for f in more:
                f(slab[i])
            pe.drain().then_inc(slab_used[i], 1)

        def pe_linear(e, slabs, tiles, nkt, stride, x, width=S):
            turn = 2 if tiles % 2 == 0 else 4
            if slabs > turn:
                with repeat(e.eng, slabs // turn, [(e.slab, turn), (e.acc, turn * tiles)]):
                    for _ in range(turn):
                        pe_slab(e, range(tiles), nkt, stride, x, width)
                slabs %= turn
            for _ in range(slabs):
                pe_slab(e, range(tiles), nkt, stride, x, width)

        def pe_token_major(e, sl, x, nkt, at, stride, cols, nb=NB, together=False):
            pe = e.eng
            s = None
            for b in range(nb):
                if not together or b == 0:
                    s = e.give(acc, e.acc)
                o = b * cols if together else 0
                for k in range(nkt):
                    mm = pe.matmul(bank[s][:, o:o + cols], x[:, k, b * P:(b + 1) * P],
                                   sl[:, k * stride + at:k * stride + at + cols], start=k == 0, stop=k == nkt - 1)
                if not together or b == nb - 1:
                    mm.then_inc(acc.full[s], 1)

        def pe_swap(e, x, tiles, wait=True):
            pe = e.eng
            for j in range(tiles):
                if wait:
                    pe.wait_ge(normed, e.nth(normed))
                s = e.give(acc, e.acc)
                pe.matmul(bank[s][:, :], K("swap"), x[:, j, :], start=True, stop=True).then_inc(acc.full[s], 1)

        def pe_ffn(e, hid):
            pe_linear(e, 11, 4, KT, 512, lambda k: xn[:, k, :])
            e.stage_end("ffn_up")
            pe_linear(e, 8, 1, FT, P, lambda k: hid[:, k, :])

        def act_square(e, src, tiles, width=S):
            e.eng.activation(sq[:, 0:tiles, 0:width], src, ACT.Square).then_inc(squared, 1)

        def act_root(e, cols, scale):
            act = e.eng
            s = e.take(acc, e.acc)
            act.activation(root[:, 0:cols], bank[s][:, 0:cols], ACT.Sqrt, scale=scale,
                           bias=small[:, 120:121]).then_inc(rooted, 1)
            act.drain().then_inc(acc.free[s], 1)

        def act_norm(e, src, width=S):
            act_square(e, src, KT, width)
            act_root(e, width // P, 1.0 / D)

        def act_copy(e, dst, width=S, scale=1.0, extra=None):
            s = e.take(acc, e.acc)
            e.eng.activation(dst, bank[s][:, 0:width], ACT.Copy, scale=scale).then_inc(acc.free[s], 1)

        def act_ffn(e):
            def turn(tiles):
                for _ in range(tiles):
                    s = e.take(acc, e.acc)
                    g = e.give(sgr, e.sg)
                    e.eng.activation(sg[g], bank[s][:, :], ACT.Silu).then_inc(sgr.full[g], 1)
                    e.eng.drain().then_inc(acc.free[s], 1)
                    e.acc.next()
            with repeat(e.eng, 5, [(e.acc, 8), (e.sg, 4)]):
                turn(4)
            turn(2)
            e.stage_end("ffn_up")

        def dve_invert(e, cols, factor=1.0, some=None):
            dve = e.eng
            dve.wait_ge(rooted, e.nth(rooted))
            e.acc.next()
            r = dve.reciprocal(inv[:, 0:cols], root[:, 0:cols])
            if some is not None:
                e.link(r, dve_step)
                r = dve.tensor_scalar(inv[:, 0:some], inv[:, 0:some], factor, None, ALU.mult)
            r.then_inc(inverted, 1)

        def dve_norm(e, src, gain, dst, shift=None, width=S, permute=False):
            dve = e.eng
            dve_invert(e, width // P)
            s = e.take(acc, e.acc)

            def nat(v):
                return v.rearrange("p (l c) -> p l c", c=4) if permute else v

            def per(v):
                return v.rearrange("p (c l) -> p l c", c=4) if permute else v

            for k in range(KT):
                last = dve.scalar_tensor_tensor(out=per(dst[:, k, 0:width]), in0=nat(src[:, k, 0:width]),
                                                scalar=gain[:, k:k + 1], in1=nat(bank[s][:, 0:width]),
                                                op0=ALU.mult, op1=ALU.mult)
            last.then_inc(acc.free[s], 1)
            if shift is not None:
                dve.drain()
                for k in range(KT):
                    dve.tensor_scalar(dst[:, k, 0:width], dst[:, k, 0:width], shift[:, k:k + 1], None, ALU.add)

        def dve_add_normed(e, src, gain):
            dve = e.eng
            dve_invert(e, NB)
            s = e.take(acc, e.acc)
            for k in range(KT):
                last = dve.scalar_tensor_tensor(out=sq[:, k, :], in0=src[:, k, :], scalar=gain[:, k:k + 1],
                                                in1=bank[s][:, :], op0=ALU.mult, op1=ALU.mult)
            last.then_inc(acc.free[s], 1)
            dve.drain()
            for k in range(KT):
                dve.tensor_tensor(h[:, k, :], h[:, k, :], sq[:, k, :], ALU.add)

        def dve_residual(e, gate, permute=False):
            for k in range(KT):
                s = e.take(acc, e.acc)
                b, hh = bank[s][:, :], h[:, k, :]
                if permute:
                    b, hh = b.rearrange("p (c l) -> p l c", c=4), hh.rearrange("p (l c) -> p l c", c=4)
                e.eng.scalar_tensor_tensor(out=hh, in0=b, scalar=gate[:, k:k + 1], in1=hh, op0=ALU.mult,
                                           op1=ALU.add).then_inc(acc.free[s], 1)

        def dve_ffn(e):
            def turn(tiles, at):
                for t in range(tiles):
                    e.acc.next()
                    g = e.take(sgr, e.sg)
                    s = e.take(acc, e.acc)
                    e.eng.tensor_tensor(hid[:, at + t, :], sg[g], bank[s][:, :], ALU.mult).then_inc(sgr.free[g], 1)
                    e.eng.drain().then_inc(acc.free[s], 1)
            with repeat(e.eng, 5, [(e.acc, 8), (e.sg, 4)]) as i:
                turn(4, 4 * i)
            turn(2, 20)
            e.stage_end("ffn_up")

        def dve_rope(e, x, out, tiles, cos, sin, tmp):
            dve = e.eng
            for j in range(tiles):
                s = e.take(acc, e.acc)
                dve.tensor_tensor(tmp[:, j, :], bank[s][:, :], sin, ALU.mult).then_inc(acc.free[s], 1)
                e.link(dve.tensor_tensor(out[:, j, :], x[:, j, :], cos, ALU.mult), dve_step)
                dve.tensor_tensor(out[:, j, :], out[:, j, :], tmp[:, j, :], ALU.add)

        hid = cut(work, 0, FT, S)
        sg = [cut(work, FT * S, S), cut(work, (FT + 1) * S, S)]

        dn_s = {n: cut(keep, 2048 + 32 * i, NB, 8) for i, n in enumerate(
            ("t", "abs", "exp", "ln", "g", "beta", "G", "eG", "kgs", "gl", "bG", "eb", "diff"))}
        dn_ea = cut(keep, 2048 + 32 * 13, 8)
        ktm = xn[:, 0:4, :].rearrange("p b (h d) -> p b h d", h=DH)
        vtm4 = xn[:, 4:8, :].rearrange("p b (h d) -> p b h d", h=DH)

        def four(t, at):
            return cut(t, at, DH, P)

        sqf = sq[:, :, :].rearrange("p a b -> p (a b)")
        dnX, dnY, dnA, dnN, dnL, dnD, dnQK, dnQG = (four(sqf, 512 * i) for i in range(8))
        dnRK, dnRV, dnKG, dnNW, dnVN, dnSf, dnSb = (four(work, 9856 + 512 * i) for i in range(7))
        dn = {n: sem(f"dn_{n}") for n in ("to_exp", "dec", "level", "a1", "xy", "sides", "nw", "vn", "state", "g")}

        def over(v, shape):
            return v.unsqueeze(2).to_broadcast(shape)

        def groups():
            for d in range(2):
                for c in (range(NB) if d == 0 else reversed(range(NB))):
                    yield d, c

        def pe_delta(e):
            pe = e.eng
            acc_of = lambda: e.give(acc, e.acc)
            heads = range(DH)
            pe_cols(e, sq, 8, NB, False, 1)
            for j in range(8):
                pe_spread(e, NB, 1, j)
            pe.wait_ge(normed, e.nth(normed))
            for j in range(8):
                s = acc_of()
                for b in range(NB):
                    mm = pe.transpose(bank[s][:, b * P:(b + 1) * P], b1_qkv[:, 4 + j, b * P:(b + 1) * P], ident)
                mm.then_inc(acc.full[s], 1)
            pe.wait_ge(dn["g"], e.nth(dn["g"]))
            s = acc_of()
            for b in range(NB):
                pe.matmul(bank[s][:, 8 * b:8 * b + 4], K("tri_f"), dn_s["g"][:, b, 0:4], start=True, stop=True)
                pe.matmul(bank[s][:, 8 * b + 4:8 * b + 8], K("tri_b"), dn_s["g"][:, b, 4:8], start=True, stop=True)
                mm = pe.matmul(bank[s][:, 32 + 8 * b:40 + 8 * b], K("ones"), dn_s["g"][:, b, :], start=True, stop=True)
            mm.then_inc(acc.full[s], 1)
            e.stage_end("delta_prep")
            for d, c in groups():
                tri = K("tri_f") if d == 0 else K("tri_b")
                state = dnSf if d == 0 else dnSb
                tok = slice(c * P, (c + 1) * P)

                def spread(col, rhs):
                    s = acc_of()
                    for x in heads:
                        mm = pe.matmul(bank[s][:, x * P:(x + 1) * P],
                                       col[:, c, 4 * d + x:4 * d + x + 1].to_broadcast([P, P]), rhs,
                                       start=True, stop=True)
                    mm.then_inc(acc.full[s], 1)

                def each(*prods):
                    s = acc_of()
                    for x in heads:
                        for n, (l, r) in enumerate(prods):
                            mm = pe.matmul(bank[s][:, x * P:(x + 1) * P], l(x), r(x), start=n == 0,
                                           stop=n == len(prods) - 1)
                    mm.then_inc(acc.full[s], 1)

                spread(dn_s["g"], tri)
                each((lambda x: b1_qkv[:, 4 + x, tok], lambda x: b1_qkv[:, 4 + x, tok]))
                each((lambda x: b1_qkv[:, 4 + x, tok], lambda x: b1_qkv[:, x, tok]))
                spread(dn_s["beta"], ident)
                spread(dn_s["eG"], ident)
                for lv in range(LEVELS):
                    pe.wait_ge(dn["level"], e.nth(dn["level"]))
                    if lv:
                        pe.wait_ge(dn["xy"], e.nth(dn["xy"]))
                    each((lambda x: dnL[:, x, :], lambda x: dnX[:, x, :]))
                    pe.wait_ge(dn["a1"], e.nth(dn["a1"]))
                    if lv < LEVELS - 1:
                        each((lambda x: dnY[:, x, :], lambda x: dnA[:, x, :]))
                    each((lambda x: dnA[:, x, :], lambda x: dnY[:, x, :]))
                pe.wait_ge(dn["xy"], e.nth(dn["xy"]))
                pe.wait_ge(dn["sides"], e.nth(dn["sides"]))
                each((lambda x: dnRK[:, x, :], lambda x: dnY[:, x, :]))
                pe.wait_ge(dn["nw"], e.nth(dn["nw"]))
                each((lambda x: dnY[:, x, :], lambda x: dnRV[:, x, :]), (lambda x: dnNW[:, x, :], lambda x: state[:, x, :]))
                pe.wait_ge(dn["vn"], e.nth(dn["vn"]))
                each((lambda x: state[:, x, :], lambda x: dnQG[:, x, :]), (lambda x: dnVN[:, x, :], lambda x: dnQK[:, x, :]))
                each((lambda x: dnKG[:, x, :], lambda x: dnVN[:, x, :]))
                pe.wait_ge(dn["state"], e.nth(dn["state"]))
            e.stage_end("delta")
            pe_cols(e, sq, 4, NB, False, 1)
            for j in range(4):
                pe_spread(e, NB, 1, j)
            e.stage_end("delta_out")

        def act_delta(e):
            act = e.eng
            act_square(e, b1_qkv[:, 0:8, :], 8)
            act_root(e, 32, 1.0)
            act.wait_ge(dn["to_exp"], e.nth(dn["to_exp"]))
            e.link(act.activation(dn_s["abs"], dn_s["t"], ACT.Abs), act_step)
            e.link(act.activation(dn_s["exp"], dn_s["abs"], ACT.Exp, scale=-1.0), act_step)
            act.activation(dn_ea, V("a_log"), ACT.Exp)
            act.activation(dn_s["eb"], b1_vtm[:, :, 136:144], ACT.Exp, scale=-1.0)
            act.activation(dn_s["ln"], dn_s["exp"], ACT.Ln, bias=1.0).then_inc(dn["dec"], 1)
            e.acc.pos += 8
            for j in range(8):
                s = e.take(acc, e.acc)
                dst = (ktm if j < 4 else vtm4)[:, :, j % 4, :]
                act.activation(dst, bank[s][:, :].rearrange("p (b d) -> p b d", b=NB), ACT.Copy).then_inc(acc.free[s], 1)
            act.wait_ge(dn["to_exp"], e.nth(dn["to_exp"]))
            act.activation(dn_s["eG"], dn_s["G"], ACT.Exp)
            act.activation(dn_s["gl"], dn_s["gl"], ACT.Exp)
            act.activation(dn_s["kgs"], dn_s["diff"], ACT.Exp).then_inc(dn["dec"], 1)
            e.stage_end("delta_prep")
            for d, c in groups():
                act.wait_ge(dn["to_exp"], e.nth(dn["to_exp"]))
                act.activation(dnD, dnD, ACT.Exp).then_inc(dn["dec"], 1)
                e.acc.pos += 5 + 3 * LEVELS - 1
                s = e.take(acc, e.acc)
                act.activation(dnNW.rearrange("p h d -> p (h d)"), bank[s][:, :], ACT.Copy, scale=-1.0)\
                    .then_inc(dn["nw"], 1)
                act.drain().then_inc(acc.free[s], 1)
                s = e.take(acc, e.acc)
                act.activation(dnVN.rearrange("p h d -> p (h d)"), bank[s][:, :], ACT.Copy).then_inc(dn["vn"], 1)
                act.drain().then_inc(acc.free[s], 1)
                e.acc.pos += 2
            e.stage_end("delta")
            act_square(e, y[:, 4:8, :], 4)
            act_root(e, 16, 1.0 / P)
            e.stage_end("delta_out")

        def dve_delta(e):
            dve = e.eng
            tt = dve.tensor_tensor
            shape = [P, NB, 8]
            tt(dn_s["t"], b1_vtm[:, :, 128:136], V("dt_bias").unsqueeze(1).to_broadcast(shape), ALU.add)\
                .then_inc(dn["to_exp"], 1)
            dve.memset(dnSf, 0.0)
            dve.memset(dnSb, 0.0)
            dve.wait_ge(dn["dec"], e.nth(dn["dec"]))
            e.link(dve.scalar_tensor_tensor(out=dn_s["ln"], in0=dn_s["t"], scalar=0.0, in1=dn_s["ln"], op0=ALU.max,
                                            op1=ALU.add), dve_step)
            dve.scalar_tensor_tensor(out=dn_s["g"], in0=dn_s["ln"], scalar=-1.0,
                                     in1=dn_ea.unsqueeze(1).to_broadcast(shape), op0=ALU.mult,
                                     op1=ALU.mult).then_inc(dn["g"], 1)
            e.link(dve.tensor_scalar(dn_s["eb"], dn_s["eb"], 1.0, None, ALU.add), dve_step)
            dve.reciprocal(dn_s["beta"], dn_s["eb"])
            dve_invert(e, 32, float(P) ** -0.5, 16)
            for j in range(8):
                s = e.take(acc, e.acc)
                last = tt(b1_qkv[:, j, :], b1_qkv[:, j, :], bank[s][:, :], ALU.mult)
                last.then_inc(acc.free[s], 1)
            dve.drain().then_inc(normed, 1)
            e.acc.pos += 8
            s = e.take(acc, e.acc)
            dve.tensor_copy(dn_s["G"], bank[s][:, 0:32].rearrange("p (b x) -> p b x", b=NB))
            e.link(dve.tensor_copy(dn_s["gl"], bank[s][:, 32:64].rearrange("p (b x) -> p b x", b=NB)), dve_step)
            tt(dn_s["diff"], dn_s["gl"], dn_s["G"], ALU.subtract).then_inc(dn["to_exp"], 1)
            dve.drain().then_inc(acc.free[s], 1)
            dve.wait_ge(dn["dec"], e.nth(dn["dec"]))
            tt(dn_s["bG"], dn_s["beta"], dn_s["eG"], ALU.mult)
            e.stage_end("delta_prep")
            full = [P, DH, P]
            for n, (d, c) in enumerate(groups()):
                tri = K("tri_f") if d == 0 else K("tri_b")
                state = dnSf if d == 0 else dnSb
                tok = slice(c * P, (c + 1) * P)
                hs = slice(4 * d, 4 * d + 4)

                def flat(s):
                    return bank[s][:, :].rearrange("p (h i) -> p h i", h=DH)

                s = e.take(acc, e.acc)
                for x in range(DH):
                    last = dve.tensor_scalar(dnD[:, x, :], bank[s][:, x * P:(x + 1) * P],
                                             dn_s["G"][:, c, 4 * d + x:4 * d + x + 1], 0.0, ALU.subtract, ALU.min)
                last.then_inc(dn["to_exp"], 1)
                dve.drain().then_inc(acc.free[s], 1)
                dve.tensor_copy(dnX, ident.unsqueeze(1).to_broadcast(full))
                dve.tensor_copy(dnY, ident.unsqueeze(1).to_broadcast(full))
                tt(dnRK, ktm[:, c], over(dn_s["bG"][:, c, hs], full), ALU.mult)
                tt(dnRV, vtm4[:, c], over(dn_s["beta"][:, c, hs], full), ALU.mult)
                tt(dnKG, ktm[:, c], over(dn_s["kgs"][:, c, hs], full), ALU.mult).then_inc(dn["sides"], 1)
                dve.wait_ge(dn["dec"], e.nth(dn["dec"]))
                e.link(tt(dnD, dnD, tri.unsqueeze(1).to_broadcast(full), ALU.mult), dve_step)
                s = e.take(acc, e.acc)
                e.link(tt(dnN, dnD, flat(s), ALU.mult), dve_step)
                dve.drain().then_inc(acc.free[s], 1)
                s = e.take(acc, e.acc)
                tt(dnQK, dnD, flat(s), ALU.mult).then_inc(acc.free[s], 1)
                s = e.take(acc, e.acc)
                tt(dnN, dnN, flat(s), ALU.mult).then_inc(acc.free[s], 1)
                s = e.take(acc, e.acc)
                tt(dnQG, b1_qkv[:, 0:4, tok], flat(s), ALU.mult).then_inc(acc.free[s], 1)
                dve.drain()

                def level(lv):
                    m = K("levels", 2, LEVELS, P)[:, d, lv, :]
                    tt(dnL, dnN, m.unsqueeze(1).to_broadcast(full), ALU.mult).then_inc(dn["level"], 1)

                level(0)
                for lv in range(LEVELS):
                    s = e.take(acc, e.acc)
                    dve.tensor_copy(dnA, flat(s)).then_inc(dn["a1"], 1)
                    dve.drain().then_inc(acc.free[s], 1)
                    if lv < LEVELS - 1:
                        level(lv + 1)
                        s0 = e.take(acc, e.acc)
                        s1 = e.take(acc, e.acc)
                        tt(dnX, dnX, flat(s0), ALU.subtract).then_inc(acc.free[s0], 1)
                    else:
                        s1 = e.take(acc, e.acc)
                    tt(dnY, dnY, flat(s1), ALU.subtract).then_inc(dn["xy"], 1)
                    dve.drain().then_inc(acc.free[s1], 1)
                e.acc.pos += 2
                s = e.take(acc, e.acc)
                o = y[:, 4:8, tok]
                if d == 0:
                    dve.tensor_copy(o, flat(s)).then_inc(acc.free[s], 1)
                else:
                    tt(o, o, flat(s), ALU.add).then_inc(acc.free[s], 1)
                s = e.take(acc, e.acc)
                for x in range(DH):
                    last = dve.scalar_tensor_tensor(out=state[:, x, :], in0=state[:, x, :],
                                                    scalar=dn_s["gl"][:, c, 4 * d + x:4 * d + x + 1],
                                                    in1=bank[s][:, x * P:(x + 1) * P], op0=ALU.mult, op1=ALU.add)
                last.then_inc(dn["state"], 1)
                dve.drain().then_inc(acc.free[s], 1)
            e.stage_end("delta")
            dve_invert(e, 16)
            for j in range(4):
                s = e.take(acc, e.acc)
                e.link(dve.scalar_tensor_tensor(out=y[:, 4 + j, :], in0=y[:, 4 + j, :], scalar=V("g_dn_out"),
                                                in1=bank[s][:, :], op0=ALU.mult, op1=ALU.mult), dve_step)
                tt(y[:, 4 + j, :], y[:, 4 + j, :], b1_gate[:, j, :], ALU.mult).then_inc(acc.free[s], 1)
            e.stage_end("delta_out")

        qk1 = xn

        def window_units():
            units = []
            for pair in range(4):
                kv = pair // 2
                for hh in range(2):
                    rows = slice(64 * hh, 64 * hh + 64)
                    for b in range(NB):
                        k0, k1 = max(0, b - 1), min(NB, b + 2)
                        n = (k1 - k0) * P
                        vals = [((kb - k0) * P, P, b1_vtm[:, kb, 64 * kv:64 * kv + 64], (0, 64 * hh, 64 * hh + 64, b * P),
                                 kb == k0, kb == k1 - 1) for kb in range(k0, k1)]
                        units.append(Unit(
                            [([(0, n, [(qk1[rows, pair, b * P:(b + 1) * P], qk1[rows, 4 + kv, k0 * P:k1 * P])])], n)],
                            [K("win")[:, (k0 - b + 1) * P:(k1 - b + 1) * P]], vals,
                            sink=V("attn_sink", 2 * pair + hh, 1), opens=hh == 0 and b == 0,
                            closes=hh == 1 and b == NB - 1))
            return units

        x_q = cut(work, 0, KT, S)
        x_k = cut(work, 4096, KT, MEM)
        x_v = cut(work, 6144, 2, D)
        mem_n = xn
        mem_in = cut(work, 8192, KT, MEM)

        def cross_units():
            units = []
            for hd in range(XH):
                for b in range(NB):
                    vals = [(m * P, P, x_v[:, m, hd * 256 + o * P:hd * 256 + (o + 1) * P], (o, 0, P, b * P), m == 0, m == 1)
                            for o in range(2) for m in range(2)]
                    units.append(Unit(
                        [([(0, MEM, [(x_q[:, 2 * hd + j, b * P:(b + 1) * P], x_k[:, 2 * hd + j, :]) for j in range(2)])], MEM)],
                        [K("causal")[:, 0:MEM]], vals, opens=b == 0, closes=b == NB - 1))
            return units

        d_raw = cut(work, 0, 6, S)
        d_qk = cut(work, 3072, 6, S)
        d_v = cut(work, 6144, 3, NB, P)

        def dilated_units():
            units = []
            for hh in range(2):
                rows = slice(64 * hh, 64 * hh + 64)
                for r in range(4):
                    q = slice(r * P, (r + 1) * P)
                    scores = [([(0, S, [(d_qk[rows, 0, q], d_qk[rows, 3, :])])], S)]
                    far = [((g - 1) * P, P, [(d_qk[rows, g, q], d_qk[rows, 3 + g, q])]) for g in (1, 2)]
                    vals = [(kb * P, P, d_v[:, 0, kb, 64 * hh:64 * hh + 64]) for kb in range(NB)]
                    vals += [(S + g * P, P, d_v[:, 1 + g, r, 64 * hh:64 * hh + 64]) for g in range(2)]
                    vals = [(*v, (0, 64 * hh, 64 * hh + 64, r * P), n == 0, n == 5) for n, v in enumerate(vals)]
                    units.append(Unit(scores + [(far, 2 * P)], [K("dil0", 4, S)[:, r, :], K("dil12")], vals,
                                      opens=hh == 0 and r == 0, closes=hh == 1 and r == 3))
            return units

        n_kslc = cut(keep, 0, 4, S)
        n_v = cut(keep, 2048, NB, 256)
        n_kcmp = cut(keep, 3264, 2, 32)
        n_vcmp = cut(keep, 3328, P)
        kv_cmp = cut(work, 0, 2, S)
        kv_raw = cut(work, 1024, 4, S)
        kv_tmp = cut(work, 3072, 4, S)
        kv_blk = cut(work, 5120, 2, NCMP, 32)
        kv_hid = cut(work, 7168, 4, 32)
        kv_kc = cut(work, 7296, 2, 32)
        kv_sqc = cut(work, 7360, 2, 32)
        q_raw = cut(work, 0, 4, S)
        q_rot = cut(work, 2048, 4, S)
        q_tmp = cut(work, 4096, 4, S)
        q_now = cut(work, 6144, 2, S)

        def sparse_units(kv, pair):
            units = []
            for hh in range(2):
                rows = slice(64 * hh, 64 * hh + 64)
                for b in range(NB):
                    q = slice(b * P, (b + 1) * P)
                    out = (0, 64 * hh, 64 * hh + 64, b * P)

                    def gate(branch):
                        return gates[:, b, bass.ds(16 * branch + 8 * kv + 2 * pair + hh, 1)]

                    units.append(Unit(
                        [([(0, NCMP, [(q_now[rows, 0, q], n_kcmp[rows, kv, 0:NCMP])])], NCMP)],
                        [K("cmp", NB, 32)[:, b, 0:NCMP]],
                        [(0, NCMP, n_vcmp[0:NCMP, 64 * kv:64 * kv + 64], out, True, False)],
                        least=FLOOR, floor=True, gate=gate(0), opens=hh == 0 and b == 0))
                    n = (b + 1) * P
                    for br in range(2):
                        vals = [(k * P, P, n_v[:, k, 128 * br + 64 * kv:128 * br + 64 * kv + 64], out, False,
                                 br == 1 and k == b) for k in range(b + 1)]
                        units.append(Unit(
                            [([(0, n, [(q_now[rows, 1, q], n_kslc[rows, 2 * br + kv, 0:n])])], n)],
                            [K("causal")[:, (3 - b) * P:4 * P]], vals, gate=gate(1 + br),
                            closes=br == 1 and hh == 1 and b == NB - 1))
            return units

        def pe_run(e):
            pe = e.eng
            pe.wait_ge(inputs_loaded, 64)
            e.stage_end("start")
            s = e.give(acc, e.acc)
            with repeat(pe, 20, [(e.slab, 2)]) as n:
                for x in range(2):
                    i, use = e.slab.next()
                    pe.wait_ge(slab_loaded[i], 16 * (use + 1))
                    for t in range(4):
                        for k in range(KT):
                            pe.matmul(bank[s][:, bass.ds(8 * n + 4 * x + t, 1)],
                                      slab[i][:, k * 512 + t * P:k * 512 + (t + 1) * P], cact[:, k:k + 1],
                                      start=k == 0, stop=k == KT - 1)
                    pe.drain().then_inc(slab_used[i], 1)
            pe.drain().then_inc(acc.full[s], 1)
            e.stage_end("ada")

            pe_norm(e)
            e.stage_end("mix_norm")
            for _ in range(5):
                pe_slab(e, range(4), KT, 512, lambda k: xn[:, k, :])
            pe_slab(e, range(2), KT, 512, lambda k: xn[:, k, :],
                    more=[lambda sl: pe_token_major(e, sl, xn, KT, 256, 512, 144)])
            e.stage_end("w_in")
            e.stage_end("rope_tables")
            pe_swap(e, sq, 6, wait=False)
            e.stage_end("rope")
            attend(e, window_units(), 1, None)
            e.stage_end("window")
            pe_delta(e)
            pe_linear(e, 2, 4, KT, 512, lambda k: y[:, k, :])
            e.stage_end("w_out")
            pe_norm(e)
            e.stage_end("mix_post")

            pe_norm(e, MEM)
            e.stage_end("mem_norm")
            pe_linear(e, 2, 4, KT, 512, lambda k: mem_n[:, k, 0:MEM], MEM)
            for _ in range(2):
                pe_slab(e, (), KT, 512, None, more=[lambda sl: pe_token_major(e, sl, mem_n, KT, 0, 512, 512, 2)])
            e.stage_end("w_ckv")
            pe_norm(e)
            e.stage_end("cross_norm")
            pe_linear(e, 2, 4, KT, 512, lambda k: xn[:, k, :])
            e.stage_end("w_cq")
            attend(e, cross_units(), 2, None)
            e.stage_end("cross")
            pe_linear(e, 2, 4, KT, 512, lambda k: y[:, k, :])
            e.stage_end("w_co")
            pe_norm(e)
            e.stage_end("cross_post")

            pe_norm(e)
            e.stage_end("ffn_norm")
            pe_ffn(e, hid)
            e.stage_end("ffn_down")
            pe_norm(e)
            e.stage_end("block_1")

            def ffn(name):
                pe_norm(e)
                e.stage_end("ffn_norm")
                pe_ffn(e, hid)
                e.stage_end(name)

            ffn("ffn_1")
            pe_norm(e)
            e.stage_end("dilated_norm")

            def pair():
                for g in range(3):
                    pe_slab(e, range(2), KT, 384, lambda k: xn[:, k, :],
                            more=[lambda sl: pe_token_major(e, sl, xn, KT, 256, 384, P, together=True)])
                pe_cols(e, sq, 6, NB, False, 2)
                for j in range(6):
                    pe_spread(e, NB, 2, j)
                pe_swap(e, d_raw, 6)
                pe.wait_ge(heads_ready, e.nth(heads_ready))
                attend(e, dilated_units(), 1, None)

            with repeat(pe, PAIRS // 2, e.rates(slab=6, acc=2 * 23 + 2, sc=32, tp=32, squared=2, inverted=2, normed=12,
                                                heads_ready=2, weighed=16, copied=16)):
                for _ in range(2):
                    pair()
                    pe_pass(e, 1)
            e.stage_end("dilated")
            pe_linear(e, 2, 4, KT, 512, lambda k: y[:, k, :])
            e.stage_end("dilated_out")
            ffn("ffn_2")

            pe_norm(e)
            e.stage_end("kv_norm")
            pe_slab(e, range(4), KT, 512, lambda k: xn[:, k, :])
            pe_slab(e, range(2), KT, 512, lambda k: xn[:, k, :],
                    more=[lambda sl: pe_token_major(e, sl, xn, KT, 256, 512, 256)])
            pe_cols(e, sq, 4, NB, False, 2)
            for j in range(4):
                pe_spread(e, NB, 2, j)
            pe_swap(e, kv_raw, 4)
            e.stage_end("kv")
            two = [e.give(acc, e.acc) for _ in range(2)]

            def compress(i):
                def f(sl):
                    for kv in range(2):
                        rows = slice(64 * kv, 64 * kv + 64)
                        at = 32 * i
                        for t in range(32):
                            pe.matmul(bank[two[kv]][:, at:at + NCMP], sl[rows, t * P:(t + 1) * P],
                                      kv_blk[rows, i, :, t], start=t == 0, stop=t == 31)
                return f

            pe_slab(e, (), 0, 0, None, more=[compress(0)])
            pe_slab(e, (), 0, 0, None, more=[compress(1)])
            for s in two:
                pe.drain().then_inc(acc.full[s], 1)
            pe.wait_ge(hidden_ready, 1)
            s = e.give(acc, e.acc)

            def second(sl):
                for kv in range(2):
                    pe.matmul(bank[s][:, kv * 32:kv * 32 + NCMP], sl[:, 0:P], kv_hid[:, kv, 0:NCMP], start=True, stop=True)
                for kv in range(2):
                    pe.matmul(bank[s][0:NCMP, 64 + kv * 64:128 + kv * 64], kv_hid[:, 2 + kv, 0:NCMP], sl[:, 128:192],
                              start=True, stop=True)

            pe_slab(e, (), 0, 0, None, more=[second])
            pe.drain().then_inc(acc.full[s], 1)
            pe.wait_ge(squared, e.nth(squared))
            s = e.give(acc, e.acc)
            for kv in range(2):
                mm = pe.matmul(bank[s][0:NCMP, kv:kv + 1], kv_sqc[:, kv, 0:NCMP], ones1, start=True, stop=True)
            mm.then_inc(acc.full[s], 1)
            pe.wait_ge(inverted, e.nth(inverted))
            s = e.give(acc, e.acc)
            for kv in range(2):
                mm = pe.matmul(bank[s][:, kv * 32:kv * 32 + NCMP], inv[0:NCMP, kv:kv + 1].to_broadcast([NCMP, P]),
                               ident[0:NCMP, 0:NCMP], start=True, stop=True)
            mm.then_inc(acc.full[s], 1)
            e.stage_end("compress")

            ffn("ffn_3")
            pe_norm(e)
            e.stage_end("sparse_norm")
            pe_slab(e, (), KT, 64, None, more=[lambda sl: pe_token_major(e, sl, xn, KT, 0, 64, 48, together=True)])
            e.stage_end("gates")
            for kv in range(2):
                pe_slab(e, range(4), KT, 512, lambda k: xn[:, k, :])
                pe_cols(e, sq, 4, NB, False, 2)
                for j in range(4):
                    pe_spread(e, NB, 2, j)
                pe_swap(e, q_raw, 4)
                e.stage_end("sparse_q")
                with repeat(pe, 4, e.rates(acc=4, sc=24, tp=24, weighed=24, copied=24, heads_ready=1)) as i:
                    pe.wait_ge(heads_ready, e.nth(heads_ready))
                    attend(e, sparse_units(kv, i), 1, None)
                    pe_pass(e, 3)
                e.stage_end("sparse")
            pe_linear(e, 2, 4, KT, 512, lambda k: y[:, k, :])
            e.stage_end("sparse_out")
            ffn("ffn_4")

        def act_run(e):
            act = e.eng
            act.wait_ge(inputs_loaded, 64)
            act.nop().then_inc(tp.free[0], 1)
            act.nop().then_inc(tp.free[1], 1)
            act.activation(cact, V("c_2"), ACT.Silu)
            e.stage_end("start")
            e.stage_end("ada")
            act_norm(e, h[:, :, :])
            e.stage_end("mix_norm")
            for t in range(22):
                if t < 4:
                    act_copy(e, sq[:, t, :], scale=0.125)
                elif t < 6:
                    act_copy(e, sq[:, t, :])
                elif t < 18:
                    s = e.take(acc, e.acc)
                    c = e.give(cvr, e.cv)
                    act.activation(b1_cv[c][:, 2:2 + S], bank[s][:, :], ACT.Copy).then_inc(cvr.full[c], 1)
                    act.drain().then_inc(acc.free[s], 1)
                else:
                    s = e.take(acc, e.acc)
                    act.activation(b1_gate[:, t - 18, :], bank[s][:, :], ACT.Silu).then_inc(acc.free[s], 1)
            e.stage_end("w_in")
            act.activation(b1_qkv, b1_qkv, ACT.Silu)
            act.wait_ge(angles_ready, 1)
            act.activation(b1_sin, b1_sin, ACT.Sin)
            act.activation(b1_cos, b1_cos, ACT.Sin)
            e.stage_end("rope_tables")
            e.stage_end("rope")

            def to(dst):
                return lambda o, b, i: act.activation(dst(o, i), b[:, :], ACT.Copy)

            attend(e, window_units(), 1, to(lambda o, i: y[:, i // 8, :]))
            e.stage_end("window")
            act_delta(e)
            for k in range(KT):
                act_copy(e, xn[:, k, :])
            e.stage_end("w_out")
            act_norm(e, xn[:, :, :])
            e.stage_end("mix_post")

            act.wait_ge(mem_loaded, 16)
            act_norm(e, mem_in, MEM)
            e.stage_end("mem_norm")
            for k in range(KT):
                act_copy(e, x_k[:, k, :], MEM)
            for n in range(2):
                for b in range(2):
                    act_copy(e, x_v[:, b, n * 512:(n + 1) * 512])
            e.stage_end("w_ckv")
            act_norm(e, h[:, :, :])
            e.stage_end("cross_norm")
            for k in range(KT):
                act_copy(e, x_q[:, k, :], scale=256.0 ** -0.5)
            e.stage_end("w_cq")
            attend(e, cross_units(), 2, to(lambda o, i: y[:, 2 * (i // 4) + o, :]))
            e.stage_end("cross")
            for k in range(KT):
                act_copy(e, xn[:, k, :])
            e.stage_end("w_co")
            act_norm(e, xn[:, :, :])
            e.stage_end("cross_post")

            act_norm(e, h[:, :, :])
            e.stage_end("ffn_norm")
            act_ffn(e)
            for k in range(KT):
                act_copy(e, xn[:, k, :])
            e.stage_end("ffn_down")
            act_norm(e, xn[:, :, :])
            e.stage_end("block_1")

            def ffn(name):
                act_norm(e, h[:, :, :])
                e.stage_end("ffn_norm")
                act_ffn(e)
                e.stage_end(name)

            ffn("ffn_1")
            act_norm(e, h[:, :, :])
            e.stage_end("dilated_norm")

            def pair(to_out):
                for g in range(3):
                    for j in (g, 3 + g):
                        act_copy(e, d_raw[:, j, :])
                    act_copy(e, d_v[:, g, :, :].rearrange("p b d -> p (b d)"))
                act.drain()
                act_square(e, d_raw, 6)
                act_root(e, 48, 1.0 / HALF)
                e.acc.pos += 12
                attend(e, dilated_units(), 1, to_out)

            with repeat(act, PAIRS // 2, e.rates(acc=2 * 23 + 2, sc=32, tp=32, maxed=16, pv_done=16)) as n:
                for x in range(2):
                    e.sc.pos += 16
                    pair(to(lambda o, i: y[:, 2 * n + x, :]))
                    s = e.take(acc, e.acc)
                    act.nop().then_inc(acc.free[s], 1)
            e.stage_end("dilated")
            e.stage_end("dilated_out")
            ffn("ffn_2")

            act_norm(e, h[:, :, :])
            e.stage_end("kv_norm")
            for j in range(2):
                act_copy(e, kv_cmp[:, j, :])
            for j in range(4):
                act_copy(e, kv_raw[:, j, :])
            for b in range(NB):
                act_copy(e, n_v[:, b, :], 256)
            act.drain()
            act_square(e, kv_raw, 4)
            act_root(e, 32, 1.0 / HALF)
            e.stage_end("kv")
            for kv in range(2):
                s = e.take(acc, e.acc)
                act.activation(kv_hid[:, kv:4:2, 0:NCMP],
                               bank[s][:, 0:64].rearrange("p (a b) -> p a b", a=2)[:, :, 0:NCMP],
                               ACT.Silu).then_inc(acc.free[s], 1)
            act.drain().then_inc(hidden_ready, 1)
            s = e.take(acc, e.acc)
            kc = bank[s][:, 0:64].rearrange("p (a b) -> p a b", a=2)[:, :, 0:NCMP]
            act.activation(kv_kc[:, :, 0:NCMP], kc, ACT.Copy)
            act.activation(n_vcmp[0:NCMP, :], bank[s][0:NCMP, 64:192], ACT.Copy)
            act.activation(kv_sqc[:, :, 0:NCMP], kc, ACT.Square).then_inc(squared, 1)
            act.drain().then_inc(acc.free[s], 1)
            s = e.take(acc, e.acc)
            act.activation(root[0:NCMP, 0:2], bank[s][0:NCMP, 0:2], ACT.Sqrt, scale=1.0 / P,
                           bias=small[0:NCMP, 120:121]).then_inc(rooted, 1)
            act.drain().then_inc(acc.free[s], 1)
            e.stage_end("compress")

            ffn("ffn_3")
            act_norm(e, h[:, :, :])
            e.stage_end("sparse_norm")
            s = e.take(acc, e.acc)
            act.activation(gates, bank[s][:, 0:192].rearrange("p (b g) -> p b g", b=NB), ACT.Exp, scale=-1.0)\
                .then_inc(rooted, 1)
            act.drain().then_inc(acc.free[s], 1)
            e.stage_end("gates")
            for kv in range(2):
                for j in range(4):
                    act_copy(e, q_raw[:, j, :])
                act.drain()
                act_square(e, q_raw, 4)
                act_root(e, 32, 1.0 / HALF)
                e.stage_end("sparse_q")
                with repeat(act, 4, e.rates(acc=4, tp=24, maxed=24, pv_done=24)) as i:
                    attend(e, sparse_units(kv, i), 1, to(lambda o, n: y[:, 4 * kv + i, :]))
                    for _ in range(3):
                        s = e.take(acc, e.acc)
                        act.nop().then_inc(acc.free[s], 1)
                e.stage_end("sparse")
            e.stage_end("sparse_out")
            ffn("ffn_4")

        def dve_run(e):
            dve = e.eng
            tt = dve.tensor_tensor
            dve.memset(small[:, 120:121], EPS)
            for b in b1_cv:
                dve.memset(b[:, 0:2], 0.0)
                dve.memset(b[:, S + 2:S + 4], 0.0)
            dve.drain()
            for s in (*acc.free, *sc.free, *cvr.free, *sgr.free):
                dve.nop().then_inc(s, 1)
            dve.wait_ge(inputs_loaded, 64)
            e.stage_end("start")
            s = e.take(acc, e.acc)
            e.link(tt(mod[:, :], bank[s][:, 0:160], V("b_ada"), ALU.add), dve_step)
            dve.drain().then_inc(acc.free[s], 1)
            for n, (at, g) in enumerate([(0, 0), (24, 8), (48, 16), (144, None), (72, 24), (96, 32), (120, 40)]):
                g = V("kv_norm_g_2") if g is None else V("norm_g_2", g, KT)
                dve.scalar_tensor_tensor(out=fold[:, n, 0, :], in0=mod[:, at + 8:at + 16], scalar=1.0, in1=g,
                                         op0=ALU.add, op1=ALU.mult)
                dve.tensor_copy(fold[:, n, 1, :], mod[:, at:at + 8])
                if n != 3:
                    dve.tensor_scalar(fold[:, n, 2, :], mod[:, at + 16:at + 24], 1.0, 1.0 if n in (1, 5) else 0.5,
                                      ALU.add, ALU.mult)
            e.stage_end("ada")

            dve_norm(e, h, V("g_mix_pre"), xn)
            e.stage_end("mix_norm")
            e.acc.pos += 22
            for t in range(12):
                c = e.take(cvr, e.cv)
                w = V("conv_w", CONV * t, CONV)
                out = b1_qkv[:, t, :]
                e.link(dve.tensor_scalar(out, b1_cv[c][:, 0:S], w[:, 0:1], None, ALU.mult), dve_step)
                for x in range(1, CONV):
                    ins = dve.scalar_tensor_tensor(out=out, in0=b1_cv[c][:, x:x + S], scalar=w[:, x:x + 1], in1=out,
                                                   op0=ALU.mult, op1=ALU.add)
                    if x < CONV - 1:
                        e.link(ins, dve_step)
                ins.then_inc(cvr.free[c], 1)
            for b in range(NB):
                s = e.take(acc, e.acc)
                dve.tensor_copy(b1_vtm[:, b, :], bank[s][:, 0:144]).then_inc(acc.free[s], 1)
            e.stage_end("w_in")
            pos = b1_tmp[:, 3, :]
            ang = b1_tmp[:, 2, :]
            e.link(dve.tensor_copy(pos, b1_tmp[:, 2, :].bitcast(I32)), dve_step)
            e.link(dve.tensor_scalar(ang, pos, K("freq"), None, ALU.mult), dve_step)
            c1 = 6.28125
            c2 = float(np.round((2 * np.pi - c1) * 2.0 ** 21) / 2.0 ** 21)
            c3 = float(np.float32(2 * np.pi - c1 - c2))
            magic = 1.5 * 2.0 ** 23
            turns = pos
            for dst, quarter in ((b1_sin, 0.0), (b1_cos, 0.25)):
                e.link(dve.tensor_scalar(turns, ang, float(1 / (2 * np.pi)), quarter, ALU.mult, ALU.add), dve_step)
                e.link(dve.tensor_scalar(turns, turns, magic, None, ALU.add), dve_step)
                e.link(dve.tensor_scalar(turns, turns, -magic, None, ALU.add), dve_step)
                e.link(dve.scalar_tensor_tensor(out=dst, in0=turns, scalar=-c1, in1=ang, op0=ALU.mult, op1=ALU.add), dve_step)
                e.link(dve.scalar_tensor_tensor(out=dst, in0=turns, scalar=-c2, in1=dst, op0=ALU.mult, op1=ALU.add), dve_step)
                e.link(dve.scalar_tensor_tensor(out=dst, in0=turns, scalar=-c3, in1=dst, op0=ALU.mult, op1=ALU.add), dve_step)
                if quarter:
                    e.link(dve.tensor_scalar(dst, dst, float(np.pi / 2), None, ALU.add), dve_step)
                last = dve.tensor_scalar(dst, dst, 3.1415925, -3.1415925, ALU.min, ALU.max)
                if not quarter:
                    e.link(last, dve_step)
            last.then_inc(angles_ready, 1)
            e.stage_end("rope_tables")
            e.link(dve.tensor_scalar(b1_sin, b1_sin, K("sign"), None, ALU.mult), dve_step)
            dve_rope(e, sq, xn, 6, b1_cos, b1_sin, y)
            e.stage_end("rope")
            attend(e, window_units(), 1, None)
            e.stage_end("window")
            dve_delta(e)
            e.stage_end("w_out")
            dve_add_normed(e, xn, V("g_mix_post"))
            e.stage_end("mix_post")

            dve_norm(e, mem_in, V("g_mem"), mem_n, width=MEM)
            e.stage_end("mem_norm")
            e.stage_end("w_ckv")
            dve_norm(e, h, V("g_cross_pre"), xn)
            e.stage_end("cross_norm")
            e.stage_end("w_cq")
            attend(e, cross_units(), 2, None)
            e.stage_end("cross")
            e.stage_end("w_co")
            dve_add_normed(e, xn, V("g_cross_post"))
            e.stage_end("cross_post")

            dve_norm(e, h, V("g_ffn_pre"), xn)
            e.stage_end("ffn_norm")
            dve_ffn(e)
            e.stage_end("ffn_down")
            dve_add_normed(e, xn, V("g_ffn_post"))
            e.stage_end("block_1")

            def ffn(n, name):
                dve_norm(e, h, fold[:, n, 0, :], xn, shift=fold[:, n, 1, :])
                e.stage_end("ffn_norm")
                dve_ffn(e)
                dve_residual(e, fold[:, n, 2, :])
                e.stage_end(name)

            def head_norm(x, tiles, gains, factor, some):
                dve_invert(e, 8 * tiles, factor, some)
                for j in range(tiles):
                    s = e.take(acc, e.acc)
                    dve.scalar_tensor_tensor(out=x[:, j, :], in0=x[:, j, :], scalar=gains(j), in1=bank[s][:, :],
                                             op0=ALU.mult, op1=ALU.mult).then_inc(normed, 1)
                    dve.drain().then_inc(acc.free[s], 1)

            ffn(0, "ffn_1")
            dve_norm(e, h, fold[:, 1, 0, :], xn, shift=fold[:, 1, 1, :], permute=True)
            e.stage_end("dilated_norm")

            def pair():
                e.acc.pos += 9
                head_norm(d_raw, 6, lambda j: V("a_q_gain_2", j, 1) if j < 3 else V("a_k_gain_2", j - 3, 1), 0.125, 24)
                dve_rope(e, d_raw, d_qk, 6, K("cos_p"), K("sin_p"), sq)
                dve.drain().then_inc(heads_ready, 1)
                attend(e, dilated_units(), 1, None)

            with repeat(dve, PAIRS // 2, e.rates(acc=2 * 23 + 2, sc=32, rooted=2, exped=16, dve_step=2 * (1 + 6 + 8 * 2))):
                for _ in range(2):
                    pair()
                    e.acc.pos += 2
            e.stage_end("dilated")
            dve_residual(e, fold[:, 1, 2, :], permute=True)
            e.stage_end("dilated_out")
            ffn(2, "ffn_2")

            dve_norm(e, h, fold[:, 3, 0, :], xn, shift=fold[:, 3, 1, :])
            e.stage_end("kv_norm")
            e.acc.pos += 10
            head_norm(kv_raw, 4, lambda j: V("kv_k_gain_2", 1 + j // 2, 1), 1.0, None)
            dve_rope(e, kv_raw, n_kslc, 4, K("cos_n"), K("sin_n"), kv_tmp)
            for i in range(2):
                for half in range(2):
                    at = 16 * half
                    tt(kv_blk[:, i, :, at:at + 16],
                       kv_cmp[:, i, at:at + 16 * NCMP].rearrange("p (c t) -> p c t", t=16),
                       V("cmp_pos_2", 32 * i + at, 16).unsqueeze(1).to_broadcast([P, NCMP, 16]), ALU.add)
            e.stage_end("kv")
            e.acc.pos += 4
            dve.wait_ge(rooted, e.nth(rooted))
            dve.reciprocal(inv[0:NCMP, 0:2], root[0:NCMP, 0:2]).then_inc(inverted, 1)
            s = e.take(acc, e.acc)
            dve.scalar_tensor_tensor(
                out=n_kcmp[:, :, 0:NCMP], in0=kv_kc[:, :, 0:NCMP], scalar=V("kv_k_gain_2", 0, 1),
                in1=bank[s][:, 0:64].rearrange("p (a b) -> p a b", a=2)[:, :, 0:NCMP],
                op0=ALU.mult, op1=ALU.mult).then_inc(acc.free[s], 1)
            e.stage_end("compress")

            ffn(4, "ffn_3")
            dve_norm(e, h, fold[:, 5, 0, :], xn, shift=fold[:, 5, 1, :])
            e.stage_end("sparse_norm")
            dve.wait_ge(rooted, e.nth(rooted))
            e.link(dve.tensor_scalar(gates, gates, 1.0, None, ALU.add), dve_step)
            dve.reciprocal(gates, gates)
            e.stage_end("gates")
            for kv in range(2):
                e.acc.pos += 4
                head_norm(q_raw, 4, lambda j: V("b_q_gain_2"), 0.125, 32)
                dve_rope(e, q_raw, q_rot, 4, K("cos_n"), K("sin_n"), q_tmp)
                e.stage_end("sparse_q")
                with repeat(dve, 4, e.rates(acc=4, sc=24, exped=24, dve_step=24 + 8)) as i:
                    dve.tensor_copy(q_now[:, 0, :], q_raw[:, i, :])
                    dve.tensor_copy(q_now[:, 1, :], q_rot[:, i, :])
                    dve.drain().then_inc(heads_ready, 1)
                    attend(e, sparse_units(kv, i), 1, None)
                    e.acc.pos += 4
                e.stage_end("sparse")
            dve_residual(e, fold[:, 5, 2, :])
            e.stage_end("sparse_out")
            ffn(6, "ffn_4")

        def finished(run, e):
            try:
                run(e)
            except Stop:
                pass

        at_end = {}

        @block.tensor
        def _(eng):
            e = Engine("pe", eng)
            finished(pe_run, e)
            at_end["slabs"] = e.slab.pos

        @block.scalar
        def _(eng):
            finished(act_run, Engine("act", eng))

        @block.vector
        def _(eng):
            finished(dve_run, Engine("dve", eng))

        @block.gpsimd
        def _(eng):
            e = Engine("pool", eng)
            try:
                for name, *_ in list(places):
                    e.stage_end(name)
                    if name == "mix_post":
                        eng.dma_start(mem_in, a["mem"]).then_inc(mem_loaded, 16)
            except Stop:
                pass

        @block.sync
        def _(eng):
            eng.dma_start(vec[:, :], a["vec"]).then_inc(inputs_loaded, 16)
            eng.dma_start(const[:, :], a["const"]).then_inc(inputs_loaded, 16)
            eng.dma_start(h[:, :, :], a["x"]).then_inc(inputs_loaded, 16)
            eng.dma_start(b1_tmp[:, 2, :].bitcast(I32), a["positions"]).then_inc(inputs_loaded, 16)
            seat = Seat(2)
            rows = a["weights"].rearrange("s p c -> (s p) c")
            left = at_end["slabs"]

            def load(n, cols):
                i, use = seat.next()
                eng.wait_ge(slab_used[i], use)
                eng.dma_start(slab[i][:, 0:cols], rows[bass.ds(n * P, P), 0:cols]).then_inc(slab_loaded[i], 16)

            at = 0
            for _, count, cols in STREAM:
                count = min(count, left)
                left -= count
                first = min(count, 2 if at == 0 else 0)
                for n in range(first):
                    i, use = seat.next()
                    eng.dma_start(slab[i][:, 0:cols], a["weights"][at + n, :, 0:cols]).then_inc(slab_loaded[i], 16)
                turns = (count - first) // 2
                if turns:
                    with repeat(eng, turns, [(seat, 2)]) as n:
                        load(2 * n + (at + first), cols)
                        load(2 * n + (at + first + 1), cols)
                if (count - first) % 2:
                    load(at + count - 1, cols)
                at += count
            for s in done.values():
                eng.wait_ge(s, len(places))
            eng.dma_start(a["out"], h[:, :, :]).then_inc(out_stored, 16)
            eng.wait_ge(out_stored, 16)


def inputs_of(x):
    def tiles(v):
        return np.ascontiguousarray(np.asarray(v).T.reshape(KT, P, -1).transpose(1, 0, 2))

    x = {k: np.asarray(v) for k, v in x.items()}
    return {
        "x": tiles(x["x"][0]), "mem": tiles(x["mem"][0]),
        "positions": np.ascontiguousarray(np.broadcast_to(x["positions"], (P, S))),
        "const": constants(), "vec": vectors(x), "weights": weight_stream(x),
    }


def kernel(**inputs):
    from concourse import bacc
    from concourse.bass_utils import run_bass_kernel_spmd

    arrays = inputs_of(inputs)
    nc = bacc.Bacc("TRN2", target_bir_lowering=False, num_devices=1)
    aps = {n: nc.dram_tensor(n, v.shape, mybir.dt.from_np(v.dtype), kind="ExternalInput").ap()
           for n, v in arrays.items()}
    aps["out"] = nc.dram_tensor("out", (P, KT, S), F32, kind="ExternalOutput").ap()
    two_blocks(nc, aps)
    r = run_bass_kernel_spmd(nc, [arrays], core_ids=[0])
    return r.results[0]["out"].transpose(2, 1, 0).reshape(1, S, D)
```

```python
from contextlib import ExitStack, contextmanager

import numpy as np

import concourse.bass as bass
from concourse import mybir

F32 = mybir.dt.float32
F32R = mybir.dt.float32r
I32 = mybir.dt.int32
ALU = mybir.AluOpType
ACT = mybir.ActivationFunctionType
AX_X = mybir.AxisListType.X

P = 128
D = 1024
KT = D // P
S = 512
NB = S // P
MEM = 256
EPS = 1e-6
FF = 2816
FT = FF // P
HALF = 64
NEG = -1e30
FLOOR = -1e29
LOWEST = -3e38
SLAB = 4096

AH, AKV = 8, 2
DH = 4
XH = 4
CONV = 5
H2 = 16
PAIRS = H2 // 2
NCMP = S // 16 - 1
LEVELS = 7
PARTS = 4
HID = (12, 10)

def ffn_stream(n):
    for half, tiles in enumerate(HID):
        yield f"up_{n}_{half}", tiles // 2, PARTS * D
        yield f"down_{n}_{half}", KT // 2, 2 * tiles * P


STREAM = [
    ("w_in", 6, 4096),
    ("ada", 40, 4096),
    ("w_out", 2, 4096),
    ("w_ckv", 4, 4096),
    ("w_cq", 2, 4096),
    ("w_co", 2, 4096),
    *ffn_stream(0), *ffn_stream(1),
    ("qkv", 3 * PAIRS, 3072),
    ("a_w_o", 2, 4096),
    *ffn_stream(2),
    ("w_kv", 2, 4096),
    ("phi", 2, 4096),
    ("phi2", 1, 256),
    *ffn_stream(3),
    ("gates", 1, 512),
    ("w_q", 2, 4096),
    ("b_w_o", 2, 4096),
    *ffn_stream(4),
]


def layout(sizes):
    at, out = 0, {}
    for name, n in sizes:
        out[name] = (at, n)
        at += n
    return out, at


CONST, N_CONST = layout([("ident", P), ("ones", P), ("swap", P), ("head2", 2), ("freq", 1), ("sign", 1)])
TABLES = [layout(t) for t in (
    [("tri_f", P), ("tri_b", P), ("levels", 2 * LEVELS * P), ("win", 3 * P), ("no_mask", MEM)],
    [("causal", 4 * P), ("dil0", 4 * S), ("dil12", 2 * P), ("cmp", NB * 32), ("cos_n", S), ("sin_n", S),
     ("cos_p", S), ("sin_p", S)])]
N_TABLES = max(n for _, n in TABLES)

VECS = [
    ("g_mix_pre", 8), ("g_mix_post", 8), ("g_cross_pre", 8), ("g_mem", 8), ("g_cross_post", 8),
    ("g_ffn_pre", 8), ("g_ffn_post", 8), ("g_dn_out", 1), ("conv_w", 12 * CONV),
    ("a_log", 8), ("dt_bias", 8), ("attn_sink", AH),
    ("c_2", 8), ("norm_g_2", 48), ("b_ada", 160), ("kv_norm_g_2", 8),
    ("a_q_gain_2", 3), ("a_k_gain_2", 3), ("kv_k_gain_2", 3), ("b_q_gain_2", 1), ("cmp_pos_2", 64),
]
VEC, N_VEC = layout(VECS)


def constants():
    c = np.zeros((P, N_CONST), np.float32)
    tables = np.zeros((2, P, N_TABLES), np.float32)

    def put(name, a):
        to = [(c, CONST), (tables[0], TABLES[0][0]), (tables[1], TABLES[1][0])]
        dst, where = next(x for x in to if name in x[1])
        at, n = where[name]
        dst[:, at:at + n] = np.asarray(a, np.float32).reshape(P, n)

    i, j = np.arange(P)[:, None], np.arange(P)[None, :]
    put("ident", i == j)
    put("ones", np.ones((P, P)))
    put("swap", (i // 64 == j // 64) & ((i % 64 + 32) % 64 == j % 64))
    put("head2", i // 64 == np.arange(2)[None, :])
    put("tri_f", i <= j)
    put("tri_b", i >= j)
    levels = np.zeros((P, 2, LEVELS, P))
    for n in range(LEVELS):
        b = 1 << n
        levels[:, 0, n] = ((j // b) % 2 == 1) & (i // b == j // b - 1)
        levels[:, 1, n] = ((i // b) % 2 == 1) & (j // b == i // b - 1)
    put("levels", levels)
    k = np.arange(3 * P)[None, :]
    put("win", np.where(np.abs(k - P - i) <= P, 0, NEG))
    put("causal", np.concatenate([np.zeros((P, 3 * P)), np.where(j <= i, 0, NEG)], 1))
    at = np.arange(S)
    token = 4 * (at % P) + at // P
    dil0 = np.zeros((P, 4, S))
    for r in range(4):
        back = (4 * np.arange(P) + r)[:, None] - token[None, :]
        dil0[:, r] = np.where((back >= 0) & (back <= P), 0, NEG)
    put("dil0", dil0)
    put("dil12", np.concatenate([np.where(j <= i, 0, NEG), np.where((j <= i) & ((i - j) % 4 == 0), 0, NEG)], 1))
    q = np.arange(P)[:, None, None] + P * np.arange(NB)[None, :, None]
    put("cmp", np.where(16 * np.arange(32)[None, None, :] + 31 <= q, 0, NEG))
    inv = (np.float32(10000.0) ** (-np.arange(32, dtype=np.float32) / np.float32(32))).astype(np.float32)
    inv = inv[np.arange(P) % 32]
    sign = np.where(np.arange(P) % 64 < 32, -1.0, 1.0)
    ang = (np.arange(S, dtype=np.float32)[None, :] * inv[:, None]).astype(np.float64)
    put("cos_n", np.cos(ang))
    put("sin_n", np.sin(ang) * sign[:, None])
    put("cos_p", np.cos(ang)[:, token])
    put("sin_p", (np.sin(ang) * sign[:, None])[:, token])
    put("freq", inv)
    put("sign", sign)
    return c, tables


def slabs_of(w, cols=512):
    k, n = w.shape
    t = w.reshape(k // P, P, n // cols, cols).transpose(2, 1, 0, 3)
    return t.reshape(n // cols, P, -1)


def weight_stream(x):
    def ffn(n, w_up, w_down):
        g, u = w_up[:, :FF].reshape(D, FT, P), w_up[:, FF:].reshape(D, FT, P)
        tiles = slabs_of(np.stack([g, u], 2).reshape(D, 2 * FF), P)
        at = 0
        for half, n_hid in enumerate(HID):
            parts[f"up_{n}_{half}"] = tiles[2 * at:2 * (at + n_hid)].reshape(-1, PARTS, P, D).transpose(0, 2, 1, 3)\
                .reshape(-1, P, PARTS * D)
            out = slabs_of(w_down[at * P:(at + n_hid) * P], P)
            parts[f"down_{n}_{half}"] = out.reshape(-1, 2, P, n_hid * P).transpose(0, 2, 1, 3)\
                .reshape(-1, P, 2 * n_hid * P)
            at += n_hid

    def twice(w):
        return [w[:, 0:64], w[:, 0:64], w[:, 64:128], w[:, 64:128]]

    w_in = x["w_in"][0]
    w_in = np.concatenate(
        [w_in[:, 0:512]] + twice(w_in[:, 512:640]) + [w_in[:, 768:2304], w_in[:, 2304:2816], w_in[:, 640:768],
         w_in[:, 2816:2832], np.zeros((D, 112), np.float32)], 1)
    qkv = x["a_w_qkv_2"][0].reshape(D, 3, 3, PAIRS, P).transpose(0, 3, 1, 2, 4).reshape(D, -1)
    w_kv = x["w_kv_2"].reshape(D, 3, 2, P)
    w_kv = np.concatenate([w_kv[:, 0, 0], w_kv[:, 0, 1]] + twice(w_kv[:, 1, 0]) + twice(w_kv[:, 2, 0])
                          + [w_kv[:, 1, 1], w_kv[:, 2, 1]], 1)
    phi1 = x["phi_w1_2"].reshape(2, 32, 64, P).transpose(2, 0, 1, 3).reshape(64, 2 * SLAB)
    phi1 = np.concatenate([phi1, phi1], 0).reshape(P, 2, SLAB).transpose(1, 0, 2)
    phi2 = x["phi_w2_2"].transpose(1, 0, 2).reshape(P, 128)
    phi2 = np.concatenate([phi2[:, 0:64], phi2[:, 0:64], phi2[:, 64:128], phi2[:, 64:128]], 1)
    qg = x["b_w_qg_2"][0]
    gates = np.concatenate([qg[:, 1024:], np.zeros((D, 16), np.float32)], 1)
    ffn_in, ffn_out = x["ffn_w_in_2"], x["ffn_w_out_2"]
    parts = {
        "ada": np.concatenate([slabs_of(w) for w in (x["w_ada_2"][0], x["w_ada_2"][1], x["w_ada_kv_2"])]),
        "w_in": slabs_of(w_in), "w_out": slabs_of(x["w_out"][0]), "w_ckv": slabs_of(x["w_ckv"][0]),
        "w_cq": slabs_of(x["w_cq"][0]), "w_co": slabs_of(x["w_co"][0]),
        "qkv": slabs_of(qkv, 3 * P), "a_w_o": slabs_of(x["a_w_o_2"][0]),
        "w_kv": slabs_of(w_kv), "phi": phi1, "phi2": phi2[None],
        "gates": slabs_of(gates, 64), "w_q": slabs_of(qg[:, :1024]), "b_w_o": slabs_of(x["b_w_o_2"][0]),
    }
    ffn(0, x["w_gate_up"][0], x["w_down"][0])
    for n in range(4):
        ffn(n + 1, ffn_in[n // 2, n % 2], ffn_out[n // 2, n % 2])
    out = np.zeros((sum(n for _, n, _ in STREAM), P, SLAB), np.float32)
    at = 0
    for name, n, cols in STREAM:
        assert parts[name].shape == (n, P, cols), (name, parts[name].shape)
        out[at:at + n, :, :cols] = parts[name]
        at += n
    return out


def vectors(x):
    def cols(a):
        return np.asarray(a).reshape(-1, P).T

    def rows(a):
        return np.broadcast_to(np.asarray(a).reshape(1, -1), (P, a.size))

    def heads(a):
        a = np.asarray(a).reshape(-1, HALF).T
        return np.concatenate([a, a], 0)

    parts = {n: cols(x[n]) for n in ("g_mix_pre", "g_mix_post", "g_cross_pre", "g_mem", "g_cross_post",
                                     "g_ffn_pre", "g_ffn_post", "g_dn_out", "c_2", "norm_g_2", "kv_norm_g_2")}
    parts |= {n: rows(x[n]) for n in ("a_log", "dt_bias", "attn_sink")}
    parts |= {n: heads(x[n]) for n in ("a_q_gain_2", "a_k_gain_2", "kv_k_gain_2", "b_q_gain_2", "cmp_pos_2")}
    parts["conv_w"] = x["conv_w"][0].reshape(CONV, 12, P).transpose(2, 1, 0).reshape(P, -1)
    parts["b_ada"] = np.concatenate([cols(x["b_ada_2"]), cols(x["b_ada_kv_2"])], 1)
    return np.ascontiguousarray(np.concatenate([parts[n] for n, _ in VECS], 1))


class Seat:

    def __init__(self, n=1):
        self.n, self.pos, self.loop = n, 0, None

    def next(self):
        at, self.pos = self.pos, self.pos + 1
        use = at // self.n
        if self.loop is not None:
            i, per = self.loop
            use = use + i * (per // self.n)
        return at % self.n, use


@contextmanager
def repeat(eng, n, seats):
    starts = [s.pos for s, _ in seats]
    with eng.Fori(0, n) as i:
        for s, per in seats:
            assert per % s.n == 0
            s.loop = (i, per)
        yield i
    for (s, per), start in zip(seats, starts):
        assert s.pos - start == per, (s.pos, start, per)
        s.pos, s.loop = start + n * per, None


class Ring:
    def __init__(self, sem, name, n):
        self.n = n
        self.full = [sem(f"{name}_full{i}") for i in range(n)]
        self.free = [sem(f"{name}_free{i}") for i in range(n)]

    def seat(self):
        return Seat(self.n)


def two_blocks(nc, a, until=None):
    with ExitStack() as ctx:
        def sb(name, shape, dt=F32):
            return ctx.enter_context(nc.sbuf_tensor(f"{name}_sb", shape, dt))

        def sem(name):
            return ctx.enter_context(nc.semaphore(name))

        h = sb("h", [P, KT, S])
        slab = [sb(f"slab{i}", [P, SLAB]) for i in range(2)]
        const = sb("const", [P, N_CONST])
        tables = sb("tables", [P, N_TABLES])
        vec = sb("vec", [P, N_VEC])
        mod = sb("mod", [P, 160])
        fold = sb("fold", [P, 7, 3, KT])
        small = sb("small", [P, 256])
        keep = sb("keep", [P, 3456])
        with ExitStack() as mixers:
            def sb_mix(name, shape):
                return mixers.enter_context(nc.sbuf_tensor(f"{name}_sb", shape, F32))

            xn = sb_mix("xn", [P, KT, S])
            y = sb_mix("y", [P, KT, S])
            sq = sb_mix("sq", [P, KT, S])
            work = sb_mix("work", [P, 17408])
        x_hi = sb("x_hi", [P, KT, S], F32R)
        x_lo = sb("x_lo", [P, KT, S], F32R)
        w_hi = [sb(f"w_hi{i}", [P, D], F32R) for i in range(PARTS)]
        w_lo = [sb(f"w_lo{i}", [P, D], F32R) for i in range(PARTS)]
        hid_hi = sb("hid_hi", [P, HID[0], S], F32R)
        hid_lo = sb("hid_lo", [P, HID[0], S], F32R)
        sg = sb("silu_gate", [P, S])
        hid = sb("hid", [P, 2, S])
        bank = [ctx.enter_context(nc.psum_tensor(f"bank{i}", [P, S], F32)) for i in range(8)]

        def K(name, *shape):
            if name in CONST:
                (at, n), src = CONST[name], const
            else:
                where = TABLES[name not in TABLES[0][0]][0]
                (at, n), src = where[name], tables
            v = src[:, at:at + n]
            if len(shape) == 2:
                return v.rearrange("p (a b) -> p a b", a=shape[0])
            if len(shape) == 3:
                return v.rearrange("p (a b c) -> p a b c", a=shape[0], b=shape[1])
            return v

        def V(name, i=0, n=None):
            at, size = VEC[name]
            return vec[:, at + i:at + (size if n is None else i + n)]

        def cut(t, at, *shape):
            n = int(np.prod(shape))
            v = t[:, at:at + n]
            if len(shape) == 2:
                return v.rearrange("p (a b) -> p a b", a=shape[0])
            if len(shape) == 3:
                return v.rearrange("p (a b c) -> p a b c", a=shape[0], b=shape[1])
            return v

        ident, ones1 = K("ident"), K("ones")[:, 0:1]

        acc = Ring(sem, "acc", 4)
        sc = Ring(sem, "scores", 2)
        tp = Ring(sem, "turned", 2)
        cvr = Ring(sem, "conv_in", 2)
        part = Ring(sem, "weight_part", PARTS)
        score_bank, turn_bank = bank[4:6], bank[6:8]
        slab_loaded = [sem(f"slab_loaded{i}") for i in range(2)]
        slab_used = [sem(f"slab_used{i}") for i in range(2)]
        inputs_loaded = sem("inputs_loaded")
        out_stored = sem("out_stored")
        squared = sem("squared")
        rooted = sem("rooted")
        inverted = sem("inverted")
        maxed = sem("maxed")
        exped = sem("exped")
        weighed = sem("weighed")
        copied = sem("copied")
        pv_done = sem("pv_done")
        normed = sem("normed")
        heads_ready = sem("heads_ready")
        angles_ready = sem("angles_ready")
        hidden_ready = sem("hidden_ready")
        mem_loaded = sem("mem_loaded")
        squared_too = sem("squared_too")
        scaled = sem("scaled")
        x_hi_ready = sem("x_hi_ready")
        x_lo_ready = sem("x_lo_ready")
        w_hi_ready = sem("w_hi_ready")
        gate_ready = sem("gate_ready")
        product_ready = sem("product_ready")
        hid_hi_ready = sem("hid_hi_ready")
        hid_lo_ready = sem("hid_lo_ready")
        tables_loaded = sem("tables_loaded")
        dve_step = sem("dve_step")
        act_step = sem("act_step")
        done = {e: sem(f"stage_done_{e}") for e in ("pe", "act", "dve", "pool")}

        counted = {"squared": squared, "rooted": rooted, "inverted": inverted, "maxed": maxed, "exped": exped,
                   "weighed": weighed, "copied": copied, "pv_done": pv_done, "normed": normed,
                   "heads_ready": heads_ready, "w_hi_ready": w_hi_ready, "gate_ready": gate_ready,
                   "product_ready": product_ready, "hid_hi_ready": hid_hi_ready, "dve_step": dve_step, "act_step": act_step}

        class Stop(Exception):
            pass

        places = []

        class Engine:

            def __init__(self, name, eng):
                self.name, self.eng, self.stages = name, eng, 0
                self.acc, self.sc, self.tp = acc.seat(), sc.seat(), tp.seat()
                self.slab, self.cv, self.part = Seat(2), cvr.seat(), part.seat()
                self.seats = {}

            def seat(self, s):
                return self.seats.setdefault(id(s), Seat())

            def nth(self, s):
                return self.seat(s).next()[1] + 1

            def rates(self, slab=None, acc=None, sc=None, tp=None, **counts):
                named = [(self.slab, slab), (self.acc, acc), (self.sc, sc), (self.tp, tp)]
                named += [(self.seat(counted[n]), per) for n, per in counts.items()]
                return [(s, per) for s, per in named if per]

            def link(self, ins, s):
                ins.then_inc(s, 1)
                self.eng.wait_ge(s, self.nth(s))

            def stage_end(self, name):
                self.stages += 1
                self.eng.drain().then_inc(done[self.name], 1)
                for other, s in done.items():
                    if other != self.name:
                        self.eng.wait_ge(s, self.stages)
                if self.name == "pe":
                    places.append((name, self.acc.pos, self.sc.pos, self.tp.pos, self.slab.pos))
                else:
                    what, self.acc.pos, self.sc.pos, self.tp.pos, self.slab.pos = places[self.stages - 1]
                    assert what == name, (what, name)
                if name == until:
                    raise Stop

            def take(self, ring, seat):
                i, use = seat.next()
                self.eng.wait_ge(ring.full[i], use + 1)
                return i

            def give(self, ring, seat):
                i, use = seat.next()
                self.eng.wait_ge(ring.free[i], use + 1)
                return i

        block = ctx.enter_context(nc.Block())

        b1_qkv = cut(work, 0, 12, S)
        b1_vtm = cut(work, 6144, NB, 144)
        b1_cv = [cut(work, 6720, S + 4), cut(work, 6720 + 516, S + 4)]
        b1_gate = cut(keep, 0, 4, S)
        b1_tmp = cut(work, 7760, 4, S)
        b1_cos, b1_sin = b1_tmp[:, 0, :], b1_tmp[:, 1, :]
        S_SB = [cut(work, 9856, 768), cut(work, 10624, 768)]
        PR = [cut(work, 11392, 768), cut(work, 12160, 768)]
        PT = [cut(work, 12928, 1024), cut(work, 13952, 1024)]
        pt_bank = [[cut(PT_, 0, S), cut(PT_, S, S)] for PT_ in PT]

        m_col = [small[:, 0:2], small[:, 2:4]]
        neg_m = [small[:, 4:5], small[:, 5:6]]
        den = [small[:, 6:7], small[:, 7:8]]
        sink_e = [small[:, 8:9], small[:, 9:10]]
        inv_den = [small[:, 10:11], small[:, 11:12]]
        root = small[:, 16:64]
        inv = small[:, 64:112]
        cact = small[:, 112:120]
        gates = cut(keep, 3072, NB, 48)

        class Unit:

            def __init__(self, scores, masks, values, least=LOWEST, sink=None, floor=False, gate=None,
                         opens=False, closes=False):
                self.scores, self.masks, self.values = scores, masks, values
                self.least, self.sink, self.floor, self.gate = least, sink, floor, gate
                self.opens, self.closes = opens, closes
                self.n = sum(n for _, n in scores)
                self.nb = len(scores)
                chunks = {}
                for col, keys, *_ in values:
                    chunks[col] = keys
                self.chunks = sorted(chunks.items())

        def attend(e, units, out_banks, finish):
            eng = e.eng
            outs = {}
            n = len(units)
            for i in range(n + 2):
                par = i % 2
                if e.name == "pe":
                    for ahead in ((0, 1) if i == 0 else (i + 1,)):
                        if ahead >= n:
                            continue
                        for parts, _ in units[ahead].scores:
                            s = e.give(sc, e.sc)
                            for at, cols, prods in parts:
                                for x, (lhsT, rhs) in enumerate(prods):
                                    mm = eng.matmul(score_bank[s][:, at:at + cols], lhsT, rhs, start=x == 0,
                                                    stop=x == len(prods) - 1)
                            mm.then_inc(sc.full[s], 1)
                    if 1 <= i <= n:
                        u = units[i - 1]
                        eng.wait_ge(weighed, e.nth(weighed))
                        for b in range(u.nb):
                            t = e.give(tp, e.tp)
                            mine = [(c, k) for c, k in u.chunks if c // S == b] if u.nb > 1 else u.chunks
                            for x, (col, keys) in enumerate(mine):
                                mm = eng.transpose(turn_bank[t][0:keys, x * P:(x + 1) * P],
                                                   PR[1 - par][:, col:col + keys], ident)
                            mm.then_inc(tp.full[t], 1)
                    if i >= 2:
                        u = units[i - 2]
                        eng.wait_ge(copied, e.nth(copied))
                        if u.opens:
                            outs.clear()
                            for o in range(out_banks):
                                outs[o] = e.give(acc, e.acc)
                        where = {c: x for x, (c, _) in enumerate(u.chunks)}
                        for col, keys, lhsT, (o, r0, r1, c0), first, last in u.values:
                            x = where[col]
                            mm = eng.matmul(bank[outs[o]][r0:r1, c0:c0 + P], lhsT,
                                            PT[par][0:keys, x * P:(x + 1) * P], start=first, stop=last)
                        mm.then_inc(pv_done, 1)
                        if u.closes:
                            for o in range(out_banks):
                                eng.drain().then_inc(acc.full[outs[o]], 1)
                elif e.name == "dve":
                    if i < n:
                        u = units[i]
                        col = 0
                        for b, ((_, cols), mask) in enumerate(zip(u.scores, u.masks)):
                            s = e.take(sc, e.sc)
                            if e.sc.loop is not None:
                                eng.memset(small[:, 124 + b:125 + b], 0.0)
                            eng.tensor_tensor_reduce(
                                out=S_SB[par][:, col:col + cols], in0=score_bank[s][:, 0:cols], in1=mask,
                                scale=1.0, scalar=u.least, op0=ALU.add, op1=ALU.max,
                                accum_out=m_col[par][:, b:b + 1]).then_inc(sc.free[s], 1)
                            col += cols
                        eng.drain()
                        if u.nb == 2:
                            e.link(eng.tensor_tensor(m_col[par][:, 0:1], m_col[par][:, 0:1], m_col[par][:, 1:2],
                                                     ALU.max), dve_step)
                        if u.sink is not None:
                            e.link(eng.tensor_tensor(m_col[par][:, 0:1], m_col[par][:, 0:1], u.sink, ALU.max), dve_step)
                        eng.tensor_scalar(neg_m[par], m_col[par][:, 0:1], -1.0, None, ALU.mult).then_inc(maxed, 1)
                    if 1 <= i <= n:
                        u, q = units[i - 1], 1 - par
                        eng.wait_ge(exped, e.nth(exped))
                        if u.sink is not None:
                            e.link(eng.tensor_tensor(den[q], den[q], sink_e[q], ALU.add), dve_step)
                        if u.floor:
                            e.link(eng.tensor_scalar(den[q], den[q], 1e-30, None, ALU.max), dve_step)
                        e.link(eng.reciprocal(inv_den[q], den[q]), dve_step)
                        if u.gate is not None:
                            eng.tensor_scalar(PR[q][:, 0:u.n], PR[q][:, 0:u.n], inv_den[q], u.gate, ALU.mult,
                                              ALU.mult).then_inc(weighed, 1)
                        else:
                            eng.tensor_scalar(PR[q][:, 0:u.n], PR[q][:, 0:u.n], inv_den[q], None,
                                              ALU.mult).then_inc(weighed, 1)
                elif e.name == "act":
                    if i < n:
                        u = units[i]
                        eng.wait_ge(maxed, e.nth(maxed))
                        if u.sink is not None:
                            eng.activation(sink_e[par], u.sink, ACT.Exp, bias=neg_m[par])
                        eng.activation(PR[par][:, 0:u.n], S_SB[par][:, 0:u.n], ACT.Exp, bias=neg_m[par],
                                       accum_out=den[par]).then_inc(exped, 1)
                    if 1 <= i <= n:
                        u, q = units[i - 1], 1 - par
                        if i >= 3:
                            eng.wait_ge(pv_done, e.nth(pv_done))
                        for b in range(u.nb):
                            t = e.take(tp, e.tp)
                            mine = [(c, k) for c, k in u.chunks if c // S == b] if u.nb > 1 else u.chunks
                            rows = mine[0][1]
                            cp = eng.activation(pt_bank[q][b][0:rows, 0:len(mine) * P],
                                                turn_bank[t][0:rows, 0:len(mine) * P], ACT.Copy)
                            if b == u.nb - 1:
                                cp.then_inc(copied, 1)
                                eng.drain().then_inc(tp.free[t], 1)
                            else:
                                cp.then_inc(tp.free[t], 1)
                    if i >= 2 and units[i - 2].closes:
                        for o in range(out_banks):
                            s = e.take(acc, e.acc)
                            finish(o, bank[s], i - 2).then_inc(acc.free[s], 1)
            if e.name == "act":
                e.seat(pv_done).pos += 1
                eng.wait_ge(pv_done, e.nth(pv_done))

        def pe_cols(e, sqv, tiles, nb, summed, sub, also=None):
            pe = e.eng
            pe.wait_ge(squared, e.nth(squared))
            if also is not None:
                pe.wait_ge(also, e.nth(also))
            s = e.give(acc, e.acc)
            rhs = ones1 if sub == 1 else K("head2")
            for j in range(1 if summed else tiles):
                for b in range(nb):
                    at = (j * nb + b) * sub
                    inner = range(tiles) if summed else [j]
                    for x in inner:
                        mm = pe.matmul(bank[s][:, at:at + sub], sqv[:, x, b * P:(b + 1) * P], rhs,
                                       start=x == inner[0], stop=x == inner[-1])
            mm.then_inc(acc.full[s], 1)
            pe.wait_ge(inverted, e.nth(inverted))

        def pe_spread(e, nb, sub, j=0):
            pe = e.eng
            s = e.give(acc, e.acc)
            for b in range(nb):
                for x in range(sub):
                    at = (j * nb + b) * sub + x
                    r = P // sub
                    mm = pe.matmul(bank[s][x * r:(x + 1) * r, b * P:(b + 1) * P],
                                   inv[:, at:at + 1].to_broadcast([P, r]), ident, start=True, stop=True)
            mm.then_inc(acc.full[s], 1)

        def pe_pass(e, n):
            for _ in range(n):
                s = e.give(acc, e.acc)
                e.eng.matmul(bank[s][:, 0:1], ident, ones1, start=True, stop=True).then_inc(acc.full[s], 1)

        def pe_norm(e, width=S):
            pe_cols(e, sq, KT, width // P, True, 1)
            pe_spread(e, width // P, 1)

        def pe_slab(e, tiles, nkt, stride, x, width=S, cols=P, more=()):
            pe = e.eng
            i, use = e.slab.next()
            pe.wait_ge(slab_loaded[i], 16 * (use + 1))
            for t in tiles:
                s = e.give(acc, e.acc)
                for k in range(nkt):
                    mm = pe.matmul(bank[s][:, 0:width], slab[i][:, k * stride + t * P:k * stride + t * P + cols],
                                   x(k), start=k == 0, stop=k == nkt - 1)
                mm.then_inc(acc.full[s], 1)
            for f in more:
                f(slab[i])
            pe.drain().then_inc(slab_used[i], 1)

        def pe_linear(e, slabs, tiles, nkt, stride, x, width=S):
            turn = 2 if tiles % 2 == 0 else 4
            if slabs > turn:
                with repeat(e.eng, slabs // turn, [(e.slab, turn), (e.acc, turn * tiles)]):
                    for _ in range(turn):
                        pe_slab(e, range(tiles), nkt, stride, x, width)
                slabs %= turn
            for _ in range(slabs):
                pe_slab(e, range(tiles), nkt, stride, x, width)

        def pe_token_major(e, sl, x, nkt, at, stride, cols, nb=NB, together=False):
            pe = e.eng
            s = None
            for b in range(nb):
                if not together or b == 0:
                    s = e.give(acc, e.acc)
                o = b * cols if together else 0
                for k in range(nkt):
                    mm = pe.matmul(bank[s][:, o:o + cols], x[:, k, b * P:(b + 1) * P],
                                   sl[:, k * stride + at:k * stride + at + cols], start=k == 0, stop=k == nkt - 1)
                if not together or b == nb - 1:
                    mm.then_inc(acc.full[s], 1)

        def pe_swap(e, x, tiles, wait=True):
            pe = e.eng
            for j in range(tiles):
                if wait:
                    pe.wait_ge(normed, e.nth(normed))
                s = e.give(acc, e.acc)
                pe.matmul(bank[s][:, :], K("swap"), x[:, j, :], start=True, stop=True).then_inc(acc.full[s], 1)

        def pe_parts(e, tiles, nkt, hi, lo, ready=None):
            pe = e.eng
            e.slab.next()
            per = PARTS // tiles
            n = nkt // per
            for t in range(tiles):
                s = e.give(acc, e.acc)
                for x in range(per):
                    p = e.take(part, e.part)
                    for k in range(n):
                        kt = x * n + k
                        if ready is not None and t == 0:
                            pe.wait_ge(ready, e.nth(ready))
                        w = slice(k * P, (k + 1) * P)
                        pe.matmul(bank[s][:, :], w_hi[p][:, w], hi[:, kt, :], start=kt == 0, stop=False)
                        pe.matmul(bank[s][:, :], w_hi[p][:, w], lo[:, kt, :], start=False, stop=False)
                        mm = pe.matmul(bank[s][:, :], w_lo[p][:, w], hi[:, kt, :], start=False, stop=kt == nkt - 1)
                    if x < per - 1:
                        mm.then_inc(part.free[p], 1)
                mm.then_inc(acc.full[s], 1)
                pe.drain().then_inc(part.free[p], 1)

        def ffn_turns(e, half, slab, loop):
            if half == 0:
                slab(0, "first")
            with loop() as i:
                slab(4 * i + 2 * (1 - half), "mid")
                slab(4 * i + 2 * (1 - half) + 2, "mid")
            slab(HID[half] - 2, "last")

        def pe_ffn(e):
            pe_cols(e, f_sq, KT, NB, True, 1, squared_too)
            pe_spread(e, NB, 1)
            for half in range(2):
                ffn_turns(e, half, lambda at, which: pe_parts(e, 4, KT, x_hi, x_lo,
                                                              x_lo_ready if which == "first" else None),
                          lambda: repeat(e.eng, 2, [(e.slab, 2), (e.part, 8), (e.acc, 8)]))
                for n in range(KT // 2):
                    pe_parts(e, 2, HID[half], hid_hi, hid_lo, hid_lo_ready if n == 0 else None)

        def act_square(e, src, tiles, width=S):
            e.eng.activation(sq[:, 0:tiles, 0:width], src, ACT.Square).then_inc(squared, 1)

        def act_root(e, cols, scale):
            act = e.eng
            s = e.take(acc, e.acc)
            act.activation(root[:, 0:cols], bank[s][:, 0:cols], ACT.Sqrt, scale=scale,
                           bias=small[:, 120:121]).then_inc(rooted, 1)
            act.drain().then_inc(acc.free[s], 1)

        def act_norm(e, src, width=S):
            act_square(e, src, KT, width)
            act_root(e, width // P, 1.0 / D)

        def act_copy(e, dst, width=S, scale=1.0, extra=None):
            s = e.take(acc, e.acc)
            e.eng.activation(dst, bank[s][:, 0:width], ACT.Copy, scale=scale).then_inc(acc.free[s], 1)

        def act_w_hi(e, quarter, cols):
            if quarter == 0:
                i, use = e.slab.next()
                e.eng.wait_ge(slab_loaded[i], 16 * (use + 1))
                e.raw = slab[i]
            p = e.give(part, e.part)
            e.eng.activation(w_hi[p][:, 0:cols], e.raw[:, quarter * cols:(quarter + 1) * cols],
                             ACT.Copy).then_inc(w_hi_ready, 1)

        def act_ffn(e, shift):
            act = e.eng
            act.activation(f_sq[:, 0:4, :], h[:, 0:4, :], ACT.Square).then_inc(squared, 1)
            act_w_hi(e, 0, D)
            act_w_hi(e, 1, D)
            act_root(e, NB, 1.0 / D)
            e.acc.pos += 1
            for k in range(KT):
                act.wait_ge(scaled, e.nth(scaled))
                if shift is None:
                    x = act.activation(x_hi[:, k, :], f_t[:, k, :], ACT.Copy)
                else:
                    x = act.activation(x_hi[:, k, :], f_t[:, k, :], ACT.Identity, bias=shift[:, k:k + 1])
                x.then_inc(x_hi_ready, 1)

            def slab_step(half, at, which):
                down = HID[half] // 2 * P
                for pair in range(2):
                    for q in range(2):
                        if pair == 0:
                            act_w_hi(e, 2 + q, D)
                        else:
                            act_w_hi(e, q, down if which == "last" else D)
                    s = e.take(acc, e.acc)
                    e.acc.next()
                    act.activation(sg[:, :], bank[s][:, :], ACT.Silu).then_inc(gate_ready, 1)
                    act.drain().then_inc(acc.free[s], 1)
                    act.wait_ge(product_ready, e.nth(product_ready))
                    act.activation(hid_hi[:, at + pair, :], hid[:, pair, :], ACT.Copy).then_inc(hid_hi_ready, 1)

            for half in range(2):
                ffn_turns(e, half, lambda at, which: slab_step(half, at, which),
                          lambda: repeat(act, 2, [(e.slab, 2), (e.part, 8), (e.acc, 8), (e.seat(product_ready), 4)]))
                cols = HID[half] // 2 * P
                for n in range(KT // 2):
                    act_w_hi(e, 2, cols)
                    act_w_hi(e, 3, cols)
                    if n < KT // 2 - 1 or half == 0:
                        after = cols if n < KT // 2 - 1 else D
                        act_w_hi(e, 0, after)
                        act_w_hi(e, 1, after)
                e.acc.pos += KT

        def dve_invert(e, cols, factor=1.0, some=None):
            dve = e.eng
            dve.wait_ge(rooted, e.nth(rooted))
            e.acc.next()
            r = dve.reciprocal(inv[:, 0:cols], root[:, 0:cols])
            if some is not None:
                e.link(r, dve_step)
                r = dve.tensor_scalar(inv[:, 0:some], inv[:, 0:some], factor, None, ALU.mult)
            r.then_inc(inverted, 1)

        def dve_norm(e, src, gain, dst, shift=None, width=S, permute=False):
            dve = e.eng
            dve_invert(e, width // P)
            s = e.take(acc, e.acc)

            def nat(v):
                return v.rearrange("p (l c) -> p l c", c=4) if permute else v

            def per(v):
                return v.rearrange("p (c l) -> p l c", c=4) if permute else v

            for k in range(KT):
                last = dve.scalar_tensor_tensor(out=per(dst[:, k, 0:width]), in0=nat(src[:, k, 0:width]),
                                                scalar=gain[:, k:k + 1], in1=nat(bank[s][:, 0:width]),
                                                op0=ALU.mult, op1=ALU.mult)
            last.then_inc(acc.free[s], 1)
            if shift is not None:
                dve.drain()
                for k in range(KT):
                    dve.tensor_scalar(dst[:, k, 0:width], dst[:, k, 0:width], shift[:, k:k + 1], None, ALU.add)

        def dve_add_normed(e, src, gain):
            dve = e.eng
            dve_invert(e, NB)
            s = e.take(acc, e.acc)
            for k in range(KT):
                last = dve.scalar_tensor_tensor(out=sq[:, k, :], in0=src[:, k, :], scalar=gain[:, k:k + 1],
                                                in1=bank[s][:, :], op0=ALU.mult, op1=ALU.mult)
            last.then_inc(acc.free[s], 1)
            dve.drain()
            for k in range(KT):
                dve.tensor_tensor(h[:, k, :], h[:, k, :], sq[:, k, :], ALU.add)

        def dve_residual(e, gate, permute=False):
            for k in range(KT):
                s = e.take(acc, e.acc)
                b, hh = bank[s][:, :], h[:, k, :]
                if permute:
                    b, hh = b.rearrange("p (c l) -> p l c", c=4), hh.rearrange("p (l c) -> p l c", c=4)
                e.eng.scalar_tensor_tensor(out=hh, in0=b, scalar=gate[:, k:k + 1], in1=hh, op0=ALU.mult,
                                           op1=ALU.add).then_inc(acc.free[s], 1)

        def dve_w_lo(e, quarter, cols):
            dve = e.eng
            if quarter == 0:
                e.raw_at, _ = e.slab.next()
            p, _ = e.part.next()
            dve.wait_ge(w_hi_ready, e.nth(w_hi_ready))
            dve.tensor_tensor(w_lo[p][:, 0:cols], slab[e.raw_at][:, quarter * cols:(quarter + 1) * cols],
                              w_hi[p][:, 0:cols].bitcast(F32), ALU.subtract).then_inc(part.full[p], 1)
            if quarter == PARTS - 1:
                dve.drain().then_inc(slab_used[e.raw_at], 1)

        def dve_ffn(e, gain, shift, finish):
            dve = e.eng
            dve.tensor_tensor(f_sq[:, 4:8, :], h[:, 4:8, :], h[:, 4:8, :], ALU.mult).then_inc(squared_too, 1)
            dve_w_lo(e, 0, D)
            dve_w_lo(e, 1, D)
            dve_invert(e, NB)
            s = e.take(acc, e.acc)
            for i in range(KT + 2):
                if i < KT:
                    dve.scalar_tensor_tensor(out=f_t[:, i, :], in0=h[:, i, :], scalar=gain[:, i:i + 1],
                                             in1=bank[s][:, :], op0=ALU.mult, op1=ALU.mult).then_inc(scaled, 1)
                if i == KT - 1:
                    dve.drain().then_inc(acc.free[s], 1)
                if i >= 2:
                    k = i - 2
                    dve.wait_ge(x_hi_ready, e.nth(x_hi_ready))
                    if shift is None:
                        x = dve.tensor_tensor(x_lo[:, k, :], f_t[:, k, :], x_hi[:, k, :].bitcast(F32), ALU.subtract)
                    else:
                        x = dve.scalar_tensor_tensor(out=x_lo[:, k, :], in0=f_t[:, k, :], scalar=shift[:, k:k + 1],
                                                     in1=x_hi[:, k, :].bitcast(F32), op0=ALU.add, op1=ALU.subtract)
                    x.then_inc(x_lo_ready, 1)

            def slab_step(half, at, which):
                down = HID[half] // 2 * P
                for pair in range(2):
                    for q in range(2):
                        if pair == 0:
                            dve_w_lo(e, 2 + q, D)
                        else:
                            dve_w_lo(e, q, down if which == "last" else D)
                    e.acc.next()
                    s = e.take(acc, e.acc)
                    dve.wait_ge(gate_ready, e.nth(gate_ready))
                    dve.tensor_tensor(hid[:, pair, :], sg[:, :], bank[s][:, :], ALU.mult).then_inc(product_ready, 1)
                    dve.drain().then_inc(acc.free[s], 1)
                    dve.wait_ge(hid_hi_ready, e.nth(hid_hi_ready))
                    dve.tensor_tensor(hid_lo[:, at + pair, :], hid[:, pair, :], hid_hi[:, at + pair, :].bitcast(F32),
                                      ALU.subtract).then_inc(hid_lo_ready, 1)

            for half in range(2):
                ffn_turns(e, half, lambda at, which: slab_step(half, at, which),
                          lambda: repeat(dve, 2, [(e.slab, 2), (e.part, 8), (e.acc, 8), (e.seat(w_hi_ready), 8),
                                                  (e.seat(gate_ready), 4), (e.seat(hid_hi_ready), 4)]))
                cols = HID[half] // 2 * P
                for n in range(KT // 2):
                    for pair in range(2):
                        if pair == 0:
                            dve_w_lo(e, 2, cols)
                            dve_w_lo(e, 3, cols)
                        elif n < KT // 2 - 1 or half == 0:
                            after = cols if n < KT // 2 - 1 else D
                            dve_w_lo(e, 0, after)
                            dve_w_lo(e, 1, after)
                        s = e.take(acc, e.acc)
                        finish(half, 2 * n + pair, bank[s]).then_inc(acc.free[s], 1)

        def dve_rope(e, x, out, tiles, cos, sin, tmp):
            dve = e.eng
            for j in range(tiles):
                s = e.take(acc, e.acc)
                dve.tensor_tensor(tmp[:, j, :], bank[s][:, :], sin, ALU.mult).then_inc(acc.free[s], 1)
                e.link(dve.tensor_tensor(out[:, j, :], x[:, j, :], cos, ALU.mult), dve_step)
                dve.tensor_tensor(out[:, j, :], out[:, j, :], tmp[:, j, :], ALU.add)

        f_t = cut(work, 4096, KT, S)
        f_sq = cut(work, 8192, KT, S)
        ffn_out = cut(tables, 0, KT, S)

        dn_s = {n: cut(keep, 2048 + 32 * i, NB, 8) for i, n in enumerate(
            ("t", "abs", "exp", "ln", "g", "beta", "G", "eG", "kgs", "gl", "bG", "eb", "diff"))}
        dn_ea = cut(keep, 2048 + 32 * 13, 8)
        ktm = xn[:, 0:4, :].rearrange("p b (h d) -> p b h d", h=DH)
        vtm4 = xn[:, 4:8, :].rearrange("p b (h d) -> p b h d", h=DH)

        def four(t, at):
            return cut(t, at, DH, P)

        sqf = sq[:, :, :].rearrange("p a b -> p (a b)")
        dnX, dnY, dnA, dnN, dnL, dnD, dnQK, dnQG = (four(sqf, 512 * i) for i in range(8))
        dnRK, dnRV, dnKG, dnNW, dnVN, dnSf, dnSb = (four(work, 9856 + 512 * i) for i in range(7))
        dn = {n: sem(f"dn_{n}") for n in ("to_exp", "dec", "level", "a1", "xy", "sides", "nw", "vn", "state", "g")}

        def over(v, shape):
            return v.unsqueeze(2).to_broadcast(shape)

        def groups():
            for d in range(2):
                for c in (range(NB) if d == 0 else reversed(range(NB))):
                    yield d, c

        def pe_delta(e):
            pe = e.eng
            acc_of = lambda: e.give(acc, e.acc)
            heads = range(DH)
            pe_cols(e, sq, 8, NB, False, 1)
            for j in range(8):
                pe_spread(e, NB, 1, j)
            pe.wait_ge(normed, e.nth(normed))
            for j in range(8):
                s = acc_of()
                for b in range(NB):
                    mm = pe.transpose(bank[s][:, b * P:(b + 1) * P], b1_qkv[:, 4 + j, b * P:(b + 1) * P], ident)
                mm.then_inc(acc.full[s], 1)
            pe.wait_ge(dn["g"], e.nth(dn["g"]))
            s = acc_of()
            for b in range(NB):
                pe.matmul(bank[s][:, 8 * b:8 * b + 4], K("tri_f"), dn_s["g"][:, b, 0:4], start=True, stop=True)
                pe.matmul(bank[s][:, 8 * b + 4:8 * b + 8], K("tri_b"), dn_s["g"][:, b, 4:8], start=True, stop=True)
                mm = pe.matmul(bank[s][:, 32 + 8 * b:40 + 8 * b], K("ones"), dn_s["g"][:, b, :], start=True, stop=True)
            mm.then_inc(acc.full[s], 1)
            e.stage_end("delta_prep")
            mods = e.give(sc, e.sc)
            ada = iter(range(40))

            def modulate():
                n = next(ada)
                i, use = e.slab.next()
                pe.wait_ge(slab_loaded[i], 16 * (use + 1))
                for t in range(4):
                    for k in range(KT):
                        pe.matmul(bank[4 + mods][:, 4 * n + t:4 * n + t + 1],
                                  slab[i][:, k * 512 + t * P:k * 512 + (t + 1) * P], cact[:, k:k + 1],
                                  start=k == 0, stop=k == KT - 1)
                pe.drain().then_inc(slab_used[i], 1)

            for d, c in groups():
                tri = K("tri_f") if d == 0 else K("tri_b")
                state = dnSf if d == 0 else dnSb
                tok = slice(c * P, (c + 1) * P)

                def spread(col, rhs):
                    s = acc_of()
                    for x in heads:
                        mm = pe.matmul(bank[s][:, x * P:(x + 1) * P],
                                       col[:, c, 4 * d + x:4 * d + x + 1].to_broadcast([P, P]), rhs,
                                       start=True, stop=True)
                    mm.then_inc(acc.full[s], 1)

                def each(*prods):
                    s = acc_of()
                    for x in heads:
                        for n, (l, r) in enumerate(prods):
                            mm = pe.matmul(bank[s][:, x * P:(x + 1) * P], l(x), r(x), start=n == 0,
                                           stop=n == len(prods) - 1)
                    mm.then_inc(acc.full[s], 1)

                spread(dn_s["g"], tri)
                each((lambda x: b1_qkv[:, 4 + x, tok], lambda x: b1_qkv[:, 4 + x, tok]))
                each((lambda x: b1_qkv[:, 4 + x, tok], lambda x: b1_qkv[:, x, tok]))
                spread(dn_s["beta"], ident)
                spread(dn_s["eG"], ident)
                for lv in range(LEVELS):
                    pe.wait_ge(dn["level"], e.nth(dn["level"]))
                    if lv:
                        pe.wait_ge(dn["xy"], e.nth(dn["xy"]))
                    each((lambda x: dnL[:, x, :], lambda x: dnX[:, x, :]))
                    if lv < 5:
                        modulate()
                    pe.wait_ge(dn["a1"], e.nth(dn["a1"]))
                    if lv < LEVELS - 1:
                        each((lambda x: dnY[:, x, :], lambda x: dnA[:, x, :]))
                    each((lambda x: dnA[:, x, :], lambda x: dnY[:, x, :]))
                pe.wait_ge(dn["xy"], e.nth(dn["xy"]))
                pe.wait_ge(dn["sides"], e.nth(dn["sides"]))
                each((lambda x: dnRK[:, x, :], lambda x: dnY[:, x, :]))
                pe.wait_ge(dn["nw"], e.nth(dn["nw"]))
                each((lambda x: dnY[:, x, :], lambda x: dnRV[:, x, :]), (lambda x: dnNW[:, x, :], lambda x: state[:, x, :]))
                pe.wait_ge(dn["vn"], e.nth(dn["vn"]))
                each((lambda x: state[:, x, :], lambda x: dnQG[:, x, :]), (lambda x: dnVN[:, x, :], lambda x: dnQK[:, x, :]))
                each((lambda x: dnKG[:, x, :], lambda x: dnVN[:, x, :]))
                pe.wait_ge(dn["state"], e.nth(dn["state"]))
            pe.drain().then_inc(sc.full[mods], 1)
            e.stage_end("delta")
            pe_cols(e, sq, 4, NB, False, 1)
            for j in range(4):
                pe_spread(e, NB, 1, j)
            e.stage_end("delta_out")

        def act_delta(e):
            act = e.eng
            act_square(e, b1_qkv[:, 0:8, :], 8)
            act_root(e, 32, 1.0)
            act.wait_ge(dn["to_exp"], e.nth(dn["to_exp"]))
            e.link(act.activation(dn_s["abs"], dn_s["t"], ACT.Abs), act_step)
            e.link(act.activation(dn_s["exp"], dn_s["abs"], ACT.Exp, scale=-1.0), act_step)
            act.activation(dn_ea, V("a_log"), ACT.Exp)
            act.activation(dn_s["eb"], b1_vtm[:, :, 136:144], ACT.Exp, scale=-1.0)
            act.activation(dn_s["ln"], dn_s["exp"], ACT.Ln, bias=1.0).then_inc(dn["dec"], 1)
            e.acc.pos += 8
            for j in range(8):
                s = e.take(acc, e.acc)
                dst = (ktm if j < 4 else vtm4)[:, :, j % 4, :]
                act.activation(dst, bank[s][:, :].rearrange("p (b d) -> p b d", b=NB), ACT.Copy).then_inc(acc.free[s], 1)
            act.wait_ge(dn["to_exp"], e.nth(dn["to_exp"]))
            act.activation(dn_s["eG"], dn_s["G"], ACT.Exp)
            act.activation(dn_s["gl"], dn_s["gl"], ACT.Exp)
            act.activation(dn_s["kgs"], dn_s["diff"], ACT.Exp).then_inc(dn["dec"], 1)
            e.stage_end("delta_prep")
            for d, c in groups():
                act.wait_ge(dn["to_exp"], e.nth(dn["to_exp"]))
                act.activation(dnD, dnD, ACT.Exp).then_inc(dn["dec"], 1)
                e.acc.pos += 5 + 3 * LEVELS - 1
                s = e.take(acc, e.acc)
                act.activation(dnNW.rearrange("p h d -> p (h d)"), bank[s][:, :], ACT.Copy, scale=-1.0)\
                    .then_inc(dn["nw"], 1)
                act.drain().then_inc(acc.free[s], 1)
                s = e.take(acc, e.acc)
                act.activation(dnVN.rearrange("p h d -> p (h d)"), bank[s][:, :], ACT.Copy).then_inc(dn["vn"], 1)
                act.drain().then_inc(acc.free[s], 1)
                e.acc.pos += 2
            e.stage_end("delta")
            act_square(e, y[:, 4:8, :], 4)
            act_root(e, 16, 1.0 / P)
            e.stage_end("delta_out")

        def dve_delta(e):
            dve = e.eng
            tt = dve.tensor_tensor
            shape = [P, NB, 8]
            tt(dn_s["t"], b1_vtm[:, :, 128:136], V("dt_bias").unsqueeze(1).to_broadcast(shape), ALU.add)\
                .then_inc(dn["to_exp"], 1)
            dve.memset(dnSf, 0.0)
            dve.memset(dnSb, 0.0)
            dve.wait_ge(dn["dec"], e.nth(dn["dec"]))
            e.link(dve.scalar_tensor_tensor(out=dn_s["ln"], in0=dn_s["t"], scalar=0.0, in1=dn_s["ln"], op0=ALU.max,
                                            op1=ALU.add), dve_step)
            dve.scalar_tensor_tensor(out=dn_s["g"], in0=dn_s["ln"], scalar=-1.0,
                                     in1=dn_ea.unsqueeze(1).to_broadcast(shape), op0=ALU.mult,
                                     op1=ALU.mult).then_inc(dn["g"], 1)
            e.link(dve.tensor_scalar(dn_s["eb"], dn_s["eb"], 1.0, None, ALU.add), dve_step)
            dve.reciprocal(dn_s["beta"], dn_s["eb"])
            dve_invert(e, 32, float(P) ** -0.5, 16)
            for j in range(8):
                s = e.take(acc, e.acc)
                last = tt(b1_qkv[:, j, :], b1_qkv[:, j, :], bank[s][:, :], ALU.mult)
                last.then_inc(acc.free[s], 1)
            dve.drain().then_inc(normed, 1)
            e.acc.pos += 8
            s = e.take(acc, e.acc)
            dve.tensor_copy(dn_s["G"], bank[s][:, 0:32].rearrange("p (b x) -> p b x", b=NB))
            e.link(dve.tensor_copy(dn_s["gl"], bank[s][:, 32:64].rearrange("p (b x) -> p b x", b=NB)), dve_step)
            tt(dn_s["diff"], dn_s["gl"], dn_s["G"], ALU.subtract).then_inc(dn["to_exp"], 1)
            dve.drain().then_inc(acc.free[s], 1)
            dve.wait_ge(dn["dec"], e.nth(dn["dec"]))
            tt(dn_s["bG"], dn_s["beta"], dn_s["eG"], ALU.mult)
            e.stage_end("delta_prep")
            full = [P, DH, P]
            for n, (d, c) in enumerate(groups()):
                tri = K("tri_f") if d == 0 else K("tri_b")
                state = dnSf if d == 0 else dnSb
                tok = slice(c * P, (c + 1) * P)
                hs = slice(4 * d, 4 * d + 4)

                def flat(s):
                    return bank[s][:, :].rearrange("p (h i) -> p h i", h=DH)

                s = e.take(acc, e.acc)
                for x in range(DH):
                    last = dve.tensor_scalar(dnD[:, x, :], bank[s][:, x * P:(x + 1) * P],
                                             dn_s["G"][:, c, 4 * d + x:4 * d + x + 1], 0.0, ALU.subtract, ALU.min)
                last.then_inc(dn["to_exp"], 1)
                dve.drain().then_inc(acc.free[s], 1)
                dve.tensor_copy(dnX, ident.unsqueeze(1).to_broadcast(full))
                dve.tensor_copy(dnY, ident.unsqueeze(1).to_broadcast(full))
                tt(dnRK, ktm[:, c], over(dn_s["bG"][:, c, hs], full), ALU.mult)
                tt(dnRV, vtm4[:, c], over(dn_s["beta"][:, c, hs], full), ALU.mult)
                tt(dnKG, ktm[:, c], over(dn_s["kgs"][:, c, hs], full), ALU.mult).then_inc(dn["sides"], 1)
                dve.wait_ge(dn["dec"], e.nth(dn["dec"]))
                e.link(tt(dnD, dnD, tri.unsqueeze(1).to_broadcast(full), ALU.mult), dve_step)
                s = e.take(acc, e.acc)
                e.link(tt(dnN, dnD, flat(s), ALU.mult), dve_step)
                dve.drain().then_inc(acc.free[s], 1)
                s = e.take(acc, e.acc)
                tt(dnQK, dnD, flat(s), ALU.mult).then_inc(acc.free[s], 1)
                s = e.take(acc, e.acc)
                tt(dnN, dnN, flat(s), ALU.mult).then_inc(acc.free[s], 1)
                s = e.take(acc, e.acc)
                tt(dnQG, b1_qkv[:, 0:4, tok], flat(s), ALU.mult).then_inc(acc.free[s], 1)
                dve.drain()

                def level(lv):
                    m = K("levels", 2, LEVELS, P)[:, d, lv, :]
                    tt(dnL, dnN, m.unsqueeze(1).to_broadcast(full), ALU.mult).then_inc(dn["level"], 1)

                level(0)
                for lv in range(LEVELS):
                    s = e.take(acc, e.acc)
                    dve.tensor_copy(dnA, flat(s)).then_inc(dn["a1"], 1)
                    dve.drain().then_inc(acc.free[s], 1)
                    if lv < LEVELS - 1:
                        level(lv + 1)
                        s0 = e.take(acc, e.acc)
                        s1 = e.take(acc, e.acc)
                        tt(dnX, dnX, flat(s0), ALU.subtract).then_inc(acc.free[s0], 1)
                    else:
                        s1 = e.take(acc, e.acc)
                    tt(dnY, dnY, flat(s1), ALU.subtract).then_inc(dn["xy"], 1)
                    dve.drain().then_inc(acc.free[s1], 1)
                e.acc.pos += 2
                s = e.take(acc, e.acc)
                o = y[:, 4:8, tok]
                if d == 0:
                    dve.tensor_copy(o, flat(s)).then_inc(acc.free[s], 1)
                else:
                    tt(o, o, flat(s), ALU.add).then_inc(acc.free[s], 1)
                s = e.take(acc, e.acc)
                for x in range(DH):
                    last = dve.scalar_tensor_tensor(out=state[:, x, :], in0=state[:, x, :],
                                                    scalar=dn_s["gl"][:, c, 4 * d + x:4 * d + x + 1],
                                                    in1=bank[s][:, x * P:(x + 1) * P], op0=ALU.mult, op1=ALU.add)
                last.then_inc(dn["state"], 1)
                dve.drain().then_inc(acc.free[s], 1)
            s = e.take(sc, e.sc)
            e.link(tt(mod[:, :], score_bank[s][:, 0:160], V("b_ada"), ALU.add), dve_step)
            dve.drain().then_inc(sc.free[s], 1)
            for n, (at, g) in enumerate([(0, 0), (24, 8), (48, 16), (144, None), (72, 24), (96, 32), (120, 40)]):
                g = V("kv_norm_g_2") if g is None else V("norm_g_2", g, KT)
                dve.scalar_tensor_tensor(out=fold[:, n, 0, :], in0=mod[:, at + 8:at + 16], scalar=1.0, in1=g,
                                         op0=ALU.add, op1=ALU.mult)
                dve.tensor_copy(fold[:, n, 1, :], mod[:, at:at + 8])
                if n != 3:
                    dve.tensor_scalar(fold[:, n, 2, :], mod[:, at + 16:at + 24], 1.0, 1.0 if n in (1, 5) else 0.5,
                                      ALU.add, ALU.mult)
            e.stage_end("delta")
            dve_invert(e, 16)
            for j in range(4):
                s = e.take(acc, e.acc)
                e.link(dve.scalar_tensor_tensor(out=y[:, 4 + j, :], in0=y[:, 4 + j, :], scalar=V("g_dn_out"),
                                                in1=bank[s][:, :], op0=ALU.mult, op1=ALU.mult), dve_step)
                tt(y[:, 4 + j, :], y[:, 4 + j, :], b1_gate[:, j, :], ALU.mult).then_inc(acc.free[s], 1)
            e.stage_end("delta_out")

        qk1 = xn

        def window_units():
            units = []
            for pair in range(4):
                kv = pair // 2
                for hh in range(2):
                    rows = slice(64 * hh, 64 * hh + 64)
                    for b in range(NB):
                        k0, k1 = max(0, b - 1), min(NB, b + 2)
                        n = (k1 - k0) * P
                        vals = [((kb - k0) * P, P, b1_vtm[:, kb, 64 * kv:64 * kv + 64], (0, 64 * hh, 64 * hh + 64, b * P),
                                 kb == k0, kb == k1 - 1) for kb in range(k0, k1)]
                        units.append(Unit(
                            [([(0, n, [(qk1[rows, pair, b * P:(b + 1) * P], qk1[rows, 4 + kv, k0 * P:k1 * P])])], n)],
                            [K("win")[:, (k0 - b + 1) * P:(k1 - b + 1) * P]], vals,
                            sink=V("attn_sink", 2 * pair + hh, 1), opens=hh == 0 and b == 0,
                            closes=hh == 1 and b == NB - 1))
            return units

        x_q = cut(work, 0, KT, S)
        x_k = cut(work, 4096, KT, MEM)
        x_v = cut(work, 6144, 2, D)
        mem_n = xn
        mem_in = cut(work, 8192, KT, MEM)

        def cross_units():
            units = []
            for hd in range(XH):
                for b in range(NB):
                    vals = [(m * P, P, x_v[:, m, hd * 256 + o * P:hd * 256 + (o + 1) * P], (o, 0, P, b * P), m == 0, m == 1)
                            for o in range(2) for m in range(2)]
                    units.append(Unit(
                        [([(0, MEM, [(x_q[:, 2 * hd + j, b * P:(b + 1) * P], x_k[:, 2 * hd + j, :]) for j in range(2)])], MEM)],
                        [K("no_mask")], vals, opens=b == 0, closes=b == NB - 1))
            return units

        d_raw = cut(work, 0, 6, S)
        d_qk = cut(work, 3072, 6, S)
        d_v = cut(work, 6144, 3, NB, P)

        def dilated_units():
            units = []
            for hh in range(2):
                rows = slice(64 * hh, 64 * hh + 64)
                for r in range(4):
                    q = slice(r * P, (r + 1) * P)
                    scores = [([(0, S, [(d_qk[rows, 0, q], d_qk[rows, 3, :])])], S)]
                    far = [((g - 1) * P, P, [(d_qk[rows, g, q], d_qk[rows, 3 + g, q])]) for g in (1, 2)]
                    vals = [(kb * P, P, d_v[:, 0, kb, 64 * hh:64 * hh + 64]) for kb in range(NB)]
                    vals += [(S + g * P, P, d_v[:, 1 + g, r, 64 * hh:64 * hh + 64]) for g in range(2)]
                    vals = [(*v, (0, 64 * hh, 64 * hh + 64, r * P), n == 0, n == 5) for n, v in enumerate(vals)]
                    units.append(Unit(scores + [(far, 2 * P)], [K("dil0", 4, S)[:, r, :], K("dil12")], vals,
                                      opens=hh == 0 and r == 0, closes=hh == 1 and r == 3))
            return units

        n_kslc = cut(keep, 0, 4, S)
        n_v = cut(keep, 2048, NB, 256)
        n_kcmp = cut(keep, 3264, 2, 32)
        n_vcmp = cut(keep, 3328, P)
        kv_cmp = cut(work, 0, 2, S)
        kv_raw = cut(work, 1024, 4, S)
        kv_tmp = cut(work, 3072, 4, S)
        kv_blk = cut(work, 5120, 2, NCMP, 32)
        kv_hid = cut(work, 7168, 4, 32)
        kv_kc = cut(work, 7296, 2, 32)
        kv_sqc = cut(work, 7360, 2, 32)
        q_raw = cut(work, 0, 4, S)
        q_rot = cut(work, 2048, 4, S)
        q_tmp = cut(work, 4096, 4, S)
        q_now = cut(work, 6144, 2, S)

        def sparse_units(kv, pair):
            units = []
            for hh in range(2):
                rows = slice(64 * hh, 64 * hh + 64)
                for b in range(NB):
                    q = slice(b * P, (b + 1) * P)
                    out = (0, 64 * hh, 64 * hh + 64, b * P)

                    def gate(branch):
                        return gates[:, b, bass.ds(16 * branch + 8 * kv + 2 * pair + hh, 1)]

                    units.append(Unit(
                        [([(0, NCMP, [(q_now[rows, 0, q], n_kcmp[rows, kv, 0:NCMP])])], NCMP)],
                        [K("cmp", NB, 32)[:, b, 0:NCMP]],
                        [(0, NCMP, n_vcmp[0:NCMP, 64 * kv:64 * kv + 64], out, True, False)],
                        least=FLOOR, floor=True, gate=gate(0), opens=hh == 0 and b == 0))
                    n = (b + 1) * P
                    for br in range(2):
                        vals = [(k * P, P, n_v[:, k, 128 * br + 64 * kv:128 * br + 64 * kv + 64], out, False,
                                 br == 1 and k == b) for k in range(b + 1)]
                        units.append(Unit(
                            [([(0, n, [(q_now[rows, 1, q], n_kslc[rows, 2 * br + kv, 0:n])])], n)],
                            [K("causal")[:, (3 - b) * P:4 * P]], vals, gate=gate(1 + br),
                            closes=br == 1 and hh == 1 and b == NB - 1))
            return units

        def pe_run(e):
            pe = e.eng
            pe.wait_ge(inputs_loaded, 80)
            e.stage_end("start")
            pe_norm(e)
            e.stage_end("mix_norm")
            for _ in range(5):
                pe_slab(e, range(4), KT, 512, lambda k: xn[:, k, :])
            pe_slab(e, range(2), KT, 512, lambda k: xn[:, k, :],
                    more=[lambda sl: pe_token_major(e, sl, xn, KT, 256, 512, 144)])
            e.stage_end("w_in")
            e.stage_end("rope_tables")
            pe_swap(e, sq, 6, wait=False)
            e.stage_end("rope")
            attend(e, window_units(), 1, None)
            e.stage_end("window")
            pe_delta(e)
            pe_linear(e, 2, 4, KT, 512, lambda k: y[:, k, :])
            e.stage_end("w_out")
            pe_norm(e)
            e.stage_end("mix_post")

            pe_norm(e, MEM)
            e.stage_end("mem_norm")
            pe_linear(e, 2, 4, KT, 512, lambda k: mem_n[:, k, 0:MEM], MEM)
            for _ in range(2):
                pe_slab(e, (), KT, 512, None, more=[lambda sl: pe_token_major(e, sl, mem_n, KT, 0, 512, 512, 2)])
            e.stage_end("w_ckv")
            pe_norm(e)
            e.stage_end("cross_norm")
            pe_linear(e, 2, 4, KT, 512, lambda k: xn[:, k, :])
            e.stage_end("w_cq")
            attend(e, cross_units(), 2, None)
            e.stage_end("cross")
            pe_linear(e, 2, 4, KT, 512, lambda k: y[:, k, :])
            e.stage_end("w_co")
            pe_norm(e)
            e.stage_end("cross_post")

            pe_ffn(e)
            e.stage_end("ffn_down")
            pe_norm(e)
            e.stage_end("block_1")

            def ffn(name):
                pe_ffn(e)
                e.stage_end(name)

            ffn("ffn_1")
            pe_norm(e)
            e.stage_end("dilated_norm")

            def pair():
                for g in range(3):
                    pe_slab(e, range(2), KT, 384, lambda k: xn[:, k, :],
                            more=[lambda sl: pe_token_major(e, sl, xn, KT, 256, 384, P, together=True)])
                pe_cols(e, sq, 6, NB, False, 2)
                for j in range(6):
                    pe_spread(e, NB, 2, j)
                pe_swap(e, d_raw, 6)
                pe.wait_ge(heads_ready, e.nth(heads_ready))
                attend(e, dilated_units(), 1, None)

            with repeat(pe, PAIRS // 2, e.rates(slab=6, acc=2 * 23 + 2, sc=32, tp=32, squared=2, inverted=2, normed=12,
                                                heads_ready=2, weighed=16, copied=16)):
                for _ in range(2):
                    pair()
                    pe_pass(e, 1)
            e.stage_end("dilated")
            pe_linear(e, 2, 4, KT, 512, lambda k: y[:, k, :])
            e.stage_end("dilated_out")
            ffn("ffn_2")

            pe_norm(e)
            e.stage_end("kv_norm")
            pe_slab(e, range(4), KT, 512, lambda k: xn[:, k, :])
            pe_slab(e, range(2), KT, 512, lambda k: xn[:, k, :],
                    more=[lambda sl: pe_token_major(e, sl, xn, KT, 256, 512, 256)])
            pe_cols(e, sq, 4, NB, False, 2)
            for j in range(4):
                pe_spread(e, NB, 2, j)
            pe_swap(e, kv_raw, 4)
            e.stage_end("kv")
            two = [e.give(acc, e.acc) for _ in range(2)]

            def compress(i):
                def f(sl):
                    for kv in range(2):
                        rows = slice(64 * kv, 64 * kv + 64)
                        at = 32 * i
                        for t in range(32):
                            pe.matmul(bank[two[kv]][:, at:at + NCMP], sl[rows, t * P:(t + 1) * P],
                                      kv_blk[rows, i, :, t], start=t == 0, stop=t == 31)
                return f

            pe_slab(e, (), 0, 0, None, more=[compress(0)])
            pe_slab(e, (), 0, 0, None, more=[compress(1)])
            for s in two:
                pe.drain().then_inc(acc.full[s], 1)
            pe.wait_ge(hidden_ready, 1)
            s = e.give(acc, e.acc)

            def second(sl):
                for kv in range(2):
                    pe.matmul(bank[s][:, kv * 32:kv * 32 + NCMP], sl[:, 0:P], kv_hid[:, kv, 0:NCMP], start=True, stop=True)
                for kv in range(2):
                    pe.matmul(bank[s][0:NCMP, 64 + kv * 64:128 + kv * 64], kv_hid[:, 2 + kv, 0:NCMP], sl[:, 128:192],
                              start=True, stop=True)

            pe_slab(e, (), 0, 0, None, more=[second])
            pe.drain().then_inc(acc.full[s], 1)
            pe.wait_ge(squared, e.nth(squared))
            s = e.give(acc, e.acc)
            for kv in range(2):
                mm = pe.matmul(bank[s][0:NCMP, kv:kv + 1], kv_sqc[:, kv, 0:NCMP], ones1, start=True, stop=True)
            mm.then_inc(acc.full[s], 1)
            pe.wait_ge(inverted, e.nth(inverted))
            s = e.give(acc, e.acc)
            for kv in range(2):
                mm = pe.matmul(bank[s][:, kv * 32:kv * 32 + NCMP], inv[0:NCMP, kv:kv + 1].to_broadcast([NCMP, P]),
                               ident[0:NCMP, 0:NCMP], start=True, stop=True)
            mm.then_inc(acc.full[s], 1)
            e.stage_end("compress")

            ffn("ffn_3")
            pe_norm(e)
            e.stage_end("sparse_norm")
            pe_slab(e, (), KT, 64, None, more=[lambda sl: pe_token_major(e, sl, xn, KT, 0, 64, 48, together=True)])
            e.stage_end("gates")
            for kv in range(2):
                pe_slab(e, range(4), KT, 512, lambda k: xn[:, k, :])
                pe_cols(e, sq, 4, NB, False, 2)
                for j in range(4):
                    pe_spread(e, NB, 2, j)
                pe_swap(e, q_raw, 4)
                e.stage_end("sparse_q")
                with repeat(pe, 4, e.rates(acc=4, sc=24, tp=24, weighed=24, copied=24, heads_ready=1)) as i:
                    pe.wait_ge(heads_ready, e.nth(heads_ready))
                    attend(e, sparse_units(kv, i), 1, None)
                    pe_pass(e, 3)
                e.stage_end("sparse")
            pe_linear(e, 2, 4, KT, 512, lambda k: y[:, k, :])
            e.stage_end("sparse_out")
            ffn("ffn_4")

        def act_run(e):
            act = e.eng
            act.wait_ge(inputs_loaded, 80)
            act.nop().then_inc(tp.free[0], 1)
            act.nop().then_inc(tp.free[1], 1)
            act.activation(cact, V("c_2"), ACT.Silu)
            e.stage_end("start")
            act_norm(e, h[:, :, :])
            e.stage_end("mix_norm")
            for t in range(22):
                if t < 4:
                    act_copy(e, sq[:, t, :], scale=0.125)
                elif t < 6:
                    act_copy(e, sq[:, t, :])
                elif t < 18:
                    s = e.take(acc, e.acc)
                    c = e.give(cvr, e.cv)
                    act.activation(b1_cv[c][:, 2:2 + S], bank[s][:, :], ACT.Copy).then_inc(cvr.full[c], 1)
                    act.drain().then_inc(acc.free[s], 1)
                else:
                    s = e.take(acc, e.acc)
                    act.activation(b1_gate[:, t - 18, :], bank[s][:, :], ACT.Silu).then_inc(acc.free[s], 1)
            e.stage_end("w_in")
            act.activation(b1_qkv, b1_qkv, ACT.Silu)
            act.wait_ge(angles_ready, 1)
            act.activation(b1_sin, b1_sin, ACT.Sin)
            act.activation(b1_cos, b1_cos, ACT.Sin)
            e.stage_end("rope_tables")
            e.stage_end("rope")

            def to(dst):
                return lambda o, b, i: act.activation(dst(o, i), b[:, :], ACT.Copy)

            attend(e, window_units(), 1, to(lambda o, i: y[:, i // 8, :]))
            e.stage_end("window")
            act_delta(e)
            for k in range(KT):
                act_copy(e, xn[:, k, :])
            e.stage_end("w_out")
            act_norm(e, xn[:, :, :])
            e.stage_end("mix_post")

            act.wait_ge(mem_loaded, 16)
            act_norm(e, mem_in, MEM)
            e.stage_end("mem_norm")
            for k in range(KT):
                act_copy(e, x_k[:, k, :], MEM)
            for n in range(2):
                for b in range(2):
                    act_copy(e, x_v[:, b, n * 512:(n + 1) * 512])
            e.stage_end("w_ckv")
            act_norm(e, h[:, :, :])
            e.stage_end("cross_norm")
            for k in range(KT):
                act_copy(e, x_q[:, k, :], scale=256.0 ** -0.5)
            e.stage_end("w_cq")
            attend(e, cross_units(), 2, to(lambda o, i: y[:, 2 * (i // 4) + o, :]))
            e.stage_end("cross")
            for k in range(KT):
                act_copy(e, xn[:, k, :])
            e.stage_end("w_co")
            act_norm(e, xn[:, :, :])
            e.stage_end("cross_post")

            act_ffn(e, None)
            e.stage_end("ffn_down")
            act_norm(e, ffn_out)
            e.stage_end("block_1")

            def ffn(n, name):
                act_ffn(e, fold[:, n, 1, :])
                e.stage_end(name)

            ffn(0, "ffn_1")
            act_norm(e, h[:, :, :])
            e.stage_end("dilated_norm")

            def pair(to_out):
                for g in range(3):
                    for j in (g, 3 + g):
                        act_copy(e, d_raw[:, j, :])
                    act_copy(e, d_v[:, g, :, :].rearrange("p b d -> p (b d)"))
                act.drain()
                act_square(e, d_raw, 6)
                act_root(e, 48, 1.0 / HALF)
                e.acc.pos += 12
                attend(e, dilated_units(), 1, to_out)

            with repeat(act, PAIRS // 2, e.rates(acc=2 * 23 + 2, sc=32, tp=32, maxed=16, pv_done=16)) as n:
                for x in range(2):
                    e.sc.pos += 16
                    pair(to(lambda o, i: y[:, 2 * n + x, :]))
                    s = e.take(acc, e.acc)
                    act.nop().then_inc(acc.free[s], 1)
            e.stage_end("dilated")
            e.stage_end("dilated_out")
            ffn(2, "ffn_2")

            act_norm(e, h[:, :, :])
            e.stage_end("kv_norm")
            for j in range(2):
                act_copy(e, kv_cmp[:, j, :])
            for j in range(4):
                act_copy(e, kv_raw[:, j, :])
            for b in range(NB):
                act_copy(e, n_v[:, b, :], 256)
            act.drain()
            act_square(e, kv_raw, 4)
            act_root(e, 32, 1.0 / HALF)
            e.stage_end("kv")
            for kv in range(2):
                s = e.take(acc, e.acc)
                act.activation(kv_hid[:, kv:4:2, 0:NCMP],
                               bank[s][:, 0:64].rearrange("p (a b) -> p a b", a=2)[:, :, 0:NCMP],
                               ACT.Silu).then_inc(acc.free[s], 1)
            act.drain().then_inc(hidden_ready, 1)
            s = e.take(acc, e.acc)
            kc = bank[s][:, 0:64].rearrange("p (a b) -> p a b", a=2)[:, :, 0:NCMP]
            act.activation(kv_kc[:, :, 0:NCMP], kc, ACT.Copy)
            act.activation(n_vcmp[0:NCMP, :], bank[s][0:NCMP, 64:192], ACT.Copy)
            act.activation(kv_sqc[:, :, 0:NCMP], kc, ACT.Square).then_inc(squared, 1)
            act.drain().then_inc(acc.free[s], 1)
            s = e.take(acc, e.acc)
            act.activation(root[0:NCMP, 0:2], bank[s][0:NCMP, 0:2], ACT.Sqrt, scale=1.0 / P,
                           bias=small[0:NCMP, 120:121]).then_inc(rooted, 1)
            act.drain().then_inc(acc.free[s], 1)
            e.stage_end("compress")

            ffn(4, "ffn_3")
            act_norm(e, h[:, :, :])
            e.stage_end("sparse_norm")
            s = e.take(acc, e.acc)
            act.activation(gates, bank[s][:, 0:192].rearrange("p (b g) -> p b g", b=NB), ACT.Exp, scale=-1.0)\
                .then_inc(rooted, 1)
            act.drain().then_inc(acc.free[s], 1)
            e.stage_end("gates")
            for kv in range(2):
                for j in range(4):
                    act_copy(e, q_raw[:, j, :])
                act.drain()
                act_square(e, q_raw, 4)
                act_root(e, 32, 1.0 / HALF)
                e.stage_end("sparse_q")
                with repeat(act, 4, e.rates(acc=4, tp=24, maxed=24, pv_done=24)) as i:
                    attend(e, sparse_units(kv, i), 1, to(lambda o, n: y[:, 4 * kv + i, :]))
                    for _ in range(3):
                        s = e.take(acc, e.acc)
                        act.nop().then_inc(acc.free[s], 1)
                e.stage_end("sparse")
            e.stage_end("sparse_out")
            ffn(6, "ffn_4")

        def dve_run(e):
            dve = e.eng
            tt = dve.tensor_tensor
            dve.memset(small[:, 120:121], EPS)
            for b in b1_cv:
                dve.memset(b[:, 0:2], 0.0)
                dve.memset(b[:, S + 2:S + 4], 0.0)
            dve.drain()
            for s in (*acc.free, *sc.free, *cvr.free, *part.free):
                dve.nop().then_inc(s, 1)
            dve.wait_ge(inputs_loaded, 80)
            e.stage_end("start")
            dve_norm(e, h, V("g_mix_pre"), xn)
            e.stage_end("mix_norm")
            e.acc.pos += 22
            for t in range(12):
                c = e.take(cvr, e.cv)
                w = V("conv_w", CONV * t, CONV)
                out = b1_qkv[:, t, :]
                e.link(dve.tensor_scalar(out, b1_cv[c][:, 0:S], w[:, 0:1], None, ALU.mult), dve_step)
                for x in range(1, CONV):
                    ins = dve.scalar_tensor_tensor(out=out, in0=b1_cv[c][:, x:x + S], scalar=w[:, x:x + 1], in1=out,
                                                   op0=ALU.mult, op1=ALU.add)
                    if x < CONV - 1:
                        e.link(ins, dve_step)
                ins.then_inc(cvr.free[c], 1)
            for b in range(NB):
                s = e.take(acc, e.acc)
                dve.tensor_copy(b1_vtm[:, b, :], bank[s][:, 0:144]).then_inc(acc.free[s], 1)
            e.stage_end("w_in")
            pos = b1_tmp[:, 3, :]
            ang = b1_tmp[:, 2, :]
            e.link(dve.tensor_copy(pos, b1_tmp[:, 2, :].bitcast(I32)), dve_step)
            e.link(dve.tensor_scalar(ang, pos, K("freq"), None, ALU.mult), dve_step)
            c1 = 6.28125
            c2 = float(np.round((2 * np.pi - c1) * 2.0 ** 21) / 2.0 ** 21)
            c3 = float(np.float32(2 * np.pi - c1 - c2))
            magic = 1.5 * 2.0 ** 23
            turns = pos
            for dst, quarter in ((b1_sin, 0.0), (b1_cos, 0.25)):
                e.link(dve.tensor_scalar(turns, ang, float(1 / (2 * np.pi)), quarter, ALU.mult, ALU.add), dve_step)
                e.link(dve.tensor_scalar(turns, turns, magic, None, ALU.add), dve_step)
                e.link(dve.tensor_scalar(turns, turns, -magic, None, ALU.add), dve_step)
                e.link(dve.scalar_tensor_tensor(out=dst, in0=turns, scalar=-c1, in1=ang, op0=ALU.mult, op1=ALU.add), dve_step)
                e.link(dve.scalar_tensor_tensor(out=dst, in0=turns, scalar=-c2, in1=dst, op0=ALU.mult, op1=ALU.add), dve_step)
                e.link(dve.scalar_tensor_tensor(out=dst, in0=turns, scalar=-c3, in1=dst, op0=ALU.mult, op1=ALU.add), dve_step)
                if quarter:
                    e.link(dve.tensor_scalar(dst, dst, float(np.pi / 2), None, ALU.add), dve_step)
                last = dve.tensor_scalar(dst, dst, 3.1415925, -3.1415925, ALU.min, ALU.max)
                if not quarter:
                    e.link(last, dve_step)
            last.then_inc(angles_ready, 1)
            e.stage_end("rope_tables")
            e.link(dve.tensor_scalar(b1_sin, b1_sin, K("sign"), None, ALU.mult), dve_step)
            dve_rope(e, sq, xn, 6, b1_cos, b1_sin, y)
            e.stage_end("rope")
            attend(e, window_units(), 1, None)
            e.stage_end("window")
            dve_delta(e)
            e.stage_end("w_out")
            dve_add_normed(e, xn, V("g_mix_post"))
            e.stage_end("mix_post")

            dve_norm(e, mem_in, V("g_mem"), mem_n, width=MEM)
            e.stage_end("mem_norm")
            e.stage_end("w_ckv")
            dve_norm(e, h, V("g_cross_pre"), xn)
            e.stage_end("cross_norm")
            e.stage_end("w_cq")
            attend(e, cross_units(), 2, None)
            e.stage_end("cross")
            e.stage_end("w_co")
            dve_add_normed(e, xn, V("g_cross_post"))
            e.stage_end("cross_post")

            def collect(half, k, b):
                if half == 0:
                    return dve.tensor_copy(ffn_out[:, k, :], b[:, :])
                return tt(ffn_out[:, k, :], ffn_out[:, k, :], b[:, :], ALU.add)

            dve_ffn(e, V("g_ffn_pre"), None, collect)
            e.stage_end("ffn_down")
            dve_add_normed(e, ffn_out, V("g_ffn_post"))
            e.stage_end("block_1")

            def ffn(n, name):
                dve_ffn(e, fold[:, n, 0, :], fold[:, n, 1, :],
                        lambda half, k, b: dve.scalar_tensor_tensor(
                            out=h[:, k, :], in0=b[:, :], scalar=fold[:, n, 2, k:k + 1], in1=h[:, k, :],
                            op0=ALU.mult, op1=ALU.add))
                e.stage_end(name)

            def head_norm(x, tiles, gains, factor, some):
                dve_invert(e, 8 * tiles, factor, some)
                for j in range(tiles):
                    s = e.take(acc, e.acc)
                    dve.scalar_tensor_tensor(out=x[:, j, :], in0=x[:, j, :], scalar=gains(j), in1=bank[s][:, :],
                                             op0=ALU.mult, op1=ALU.mult).then_inc(normed, 1)
                    dve.drain().then_inc(acc.free[s], 1)

            ffn(0, "ffn_1")
            dve_norm(e, h, fold[:, 1, 0, :], xn, shift=fold[:, 1, 1, :], permute=True)
            e.stage_end("dilated_norm")

            def pair():
                e.acc.pos += 9
                head_norm(d_raw, 6, lambda j: V("a_q_gain_2", j, 1) if j < 3 else V("a_k_gain_2", j - 3, 1), 0.125, 24)
                dve_rope(e, d_raw, d_qk, 6, K("cos_p"), K("sin_p"), sq)
                dve.drain().then_inc(heads_ready, 1)
                attend(e, dilated_units(), 1, None)

            with repeat(dve, PAIRS // 2, e.rates(acc=2 * 23 + 2, sc=32, rooted=2, exped=16, dve_step=2 * (1 + 6 + 8 * 2))):
                for _ in range(2):
                    pair()
                    e.acc.pos += 2
            e.stage_end("dilated")
            dve_residual(e, fold[:, 1, 2, :], permute=True)
            e.stage_end("dilated_out")
            ffn(2, "ffn_2")

            dve_norm(e, h, fold[:, 3, 0, :], xn, shift=fold[:, 3, 1, :])
            e.stage_end("kv_norm")
            e.acc.pos += 10
            head_norm(kv_raw, 4, lambda j: V("kv_k_gain_2", 1 + j // 2, 1), 1.0, None)
            dve_rope(e, kv_raw, n_kslc, 4, K("cos_n"), K("sin_n"), kv_tmp)
            for i in range(2):
                for half in range(2):
                    at = 16 * half
                    tt(kv_blk[:, i, :, at:at + 16],
                       kv_cmp[:, i, at:at + 16 * NCMP].rearrange("p (c t) -> p c t", t=16),
                       V("cmp_pos_2", 32 * i + at, 16).unsqueeze(1).to_broadcast([P, NCMP, 16]), ALU.add)
            e.stage_end("kv")
            e.acc.pos += 4
            dve.wait_ge(rooted, e.nth(rooted))
            dve.reciprocal(inv[0:NCMP, 0:2], root[0:NCMP, 0:2]).then_inc(inverted, 1)
            s = e.take(acc, e.acc)
            dve.scalar_tensor_tensor(
                out=n_kcmp[:, :, 0:NCMP], in0=kv_kc[:, :, 0:NCMP], scalar=V("kv_k_gain_2", 0, 1),
                in1=bank[s][:, 0:64].rearrange("p (a b) -> p a b", a=2)[:, :, 0:NCMP],
                op0=ALU.mult, op1=ALU.mult).then_inc(acc.free[s], 1)
            e.stage_end("compress")

            ffn(4, "ffn_3")
            dve_norm(e, h, fold[:, 5, 0, :], xn, shift=fold[:, 5, 1, :])
            e.stage_end("sparse_norm")
            dve.wait_ge(rooted, e.nth(rooted))
            e.link(dve.tensor_scalar(gates, gates, 1.0, None, ALU.add), dve_step)
            dve.reciprocal(gates, gates)
            e.stage_end("gates")
            for kv in range(2):
                e.acc.pos += 4
                head_norm(q_raw, 4, lambda j: V("b_q_gain_2"), 0.125, 32)
                dve_rope(e, q_raw, q_rot, 4, K("cos_n"), K("sin_n"), q_tmp)
                e.stage_end("sparse_q")
                with repeat(dve, 4, e.rates(acc=4, sc=24, exped=24, dve_step=24 + 8)) as i:
                    dve.tensor_copy(q_now[:, 0, :], q_raw[:, i, :])
                    dve.tensor_copy(q_now[:, 1, :], q_rot[:, i, :])
                    dve.drain().then_inc(heads_ready, 1)
                    attend(e, sparse_units(kv, i), 1, None)
                    e.acc.pos += 4
                e.stage_end("sparse")
            dve_residual(e, fold[:, 5, 2, :])
            e.stage_end("sparse_out")
            ffn(6, "ffn_4")

        def finished(run, e):
            try:
                run(e)
            except Stop:
                pass

        at_end = {}

        @block.tensor
        def _(eng):
            e = Engine("pe", eng)
            finished(pe_run, e)
            at_end["slabs"] = e.slab.pos

        @block.scalar
        def _(eng):
            finished(act_run, Engine("act", eng))

        @block.vector
        def _(eng):
            finished(dve_run, Engine("dve", eng))

        @block.gpsimd
        def _(eng):
            e = Engine("pool", eng)
            try:
                for name, *_ in list(places):
                    if name == "ffn_1":
                        eng.wait_ge(tables_loaded, 16)
                    e.stage_end(name)
                    if name == "block_1":
                        eng.dma_start(tables[:, :], a["tables"][1]).then_inc(tables_loaded, 16)
                    if name == "mix_post":
                        eng.dma_start(mem_in, a["mem"]).then_inc(mem_loaded, 16)
            except Stop:
                pass

        @block.sync
        def _(eng):
            eng.dma_start(vec[:, :], a["vec"]).then_inc(inputs_loaded, 16)
            eng.dma_start(const[:, :], a["const"]).then_inc(inputs_loaded, 16)
            eng.dma_start(tables[:, :], a["tables"][0]).then_inc(inputs_loaded, 16)
            eng.dma_start(h[:, :, :], a["x"]).then_inc(inputs_loaded, 16)
            eng.dma_start(b1_tmp[:, 2, :].bitcast(I32), a["positions"]).then_inc(inputs_loaded, 16)
            seat = Seat(2)
            rows = a["weights"].rearrange("s p c -> (s p) c")
            left = at_end["slabs"]

            def load(n, cols):
                i, use = seat.next()
                eng.wait_ge(slab_used[i], use)
                eng.dma_start(slab[i][:, 0:cols], rows[bass.ds(n * P, P), 0:cols]).then_inc(slab_loaded[i], 16)

            at = 0
            for _, count, cols in STREAM:
                count = min(count, left)
                left -= count
                first = min(count, 2 if at == 0 else 0)
                for n in range(first):
                    i, use = seat.next()
                    eng.dma_start(slab[i][:, 0:cols], a["weights"][at + n, :, 0:cols]).then_inc(slab_loaded[i], 16)
                turns = (count - first) // 2
                if turns:
                    with repeat(eng, turns, [(seat, 2)]) as n:
                        load(2 * n + (at + first), cols)
                        load(2 * n + (at + first + 1), cols)
                if (count - first) % 2:
                    load(at + count - 1, cols)
                at += count
            for s in done.values():
                eng.wait_ge(s, len(places))
            eng.dma_start(a["out"], h[:, :, :]).then_inc(out_stored, 16)
            eng.wait_ge(out_stored, 16)


def inputs_of(x):
    def tiles(v):
        return np.ascontiguousarray(np.asarray(v).T.reshape(KT, P, -1).transpose(1, 0, 2))

    x = {k: np.asarray(v) for k, v in x.items()}
    const, tables = constants()
    return {
        "x": tiles(x["x"][0]), "mem": tiles(x["mem"][0]),
        "positions": np.ascontiguousarray(np.broadcast_to(x["positions"], (P, S))),
        "const": const, "tables": tables, "vec": vectors(x), "weights": weight_stream(x),
    }


def kernel(**inputs):
    from concourse import bacc
    from concourse.bass_utils import run_bass_kernel_spmd

    arrays = inputs_of(inputs)
    nc = bacc.Bacc("TRN2", target_bir_lowering=False, num_devices=1)
    aps = {n: nc.dram_tensor(n, v.shape, mybir.dt.from_np(v.dtype), kind="ExternalInput").ap()
           for n, v in arrays.items()}
    aps["out"] = nc.dram_tensor("out", (P, KT, S), F32, kind="ExternalOutput").ap()
    two_blocks(nc, aps)
    r = run_bass_kernel_spmd(nc, [arrays], core_ids=[0])
    return r.results[0]["out"].transpose(2, 1, 0).reshape(1, S, D)
```
